# Optimizing a Trainium2 kernel written in Bass

```python
import jax, jax.numpy as jnp
from jax import lax
import numpy as np

D_MODEL = 2048
BATCH = 1
SEQ = 256
DEPTH = 1

GRID_W = 64
NA_HEAD_DIM = 64
NA_WIDTH = D_MODEL // 2
NA_HEADS = NA_WIDTH // NA_HEAD_DIM
NA_WIN_ROWS = 8
NA_WIN_COLS = 16
HG_KEY_DIM = 128
HG_VAL_DIM = 128
HG_WIDTH = D_MODEL // 2
HG_HEADS = HG_WIDTH // HG_VAL_DIM
HG_KEY_WIDTH = HG_HEADS * HG_KEY_DIM
HG_CHUNK = 64
N_BRANCHES = 2
NORM_EPS = 1e-6
IN_COLS = 4 * NA_WIDTH + 3 * HG_KEY_WIDTH + 2 * HG_WIDTH + N_BRANCHES * D_MODEL

kernel_name = "hybrid_natten_hgrn2_gated_merge_encoder"

def _rmsnorm(x, w):
    xf = x.astype(jnp.float32)
    y = xf * lax.rsqrt(jnp.mean(xf * xf, axis=-1, keepdims=True) + NORM_EPS)
    return (y * w.astype(jnp.float32)).astype(x.dtype)

def _neighbourhood_attention(q, k, v, rpb):
    B, T, H, Dh = q.shape
    rows = T // GRID_W
    wr = min(NA_WIN_ROWS, rows)
    qg = q.reshape(B, rows, GRID_W, H, Dh)
    kg = k.reshape(B, rows, GRID_W, H, Dh)
    vg = v.reshape(B, rows, GRID_W, H, Dh)
    qc = jnp.arange(GRID_W)
    kc = jnp.arange(GRID_W)
    cs = jnp.clip(qc - NA_WIN_COLS // 2, 0, GRID_W - NA_WIN_COLS)
    col_mask = (kc[None, :] >= cs[:, None]) & (kc[None, :] < cs[:, None] + NA_WIN_COLS)
    col_idx = jnp.clip(kc[None, :] - qc[:, None] + NA_WIN_COLS - 1, 0, 2 * NA_WIN_COLS - 2)
    scale = Dh ** -0.5

    def row_block(r):
        rs = jnp.clip(r - wr // 2, 0, rows - wr)
        kb = lax.dynamic_slice_in_dim(kg, rs, wr, axis=1)
        vb = lax.dynamic_slice_in_dim(vg, rs, wr, axis=1)
        qr = lax.dynamic_index_in_dim(qg, r, axis=1, keepdims=False)
        s = jnp.einsum('bqhd,bjkhd->bhqjk', qr, kb).astype(jnp.float32) * scale
        row_idx = rs + jnp.arange(wr) - r + NA_WIN_ROWS - 1
        bias = rpb[:, row_idx][:, :, col_idx]
        s = s + jnp.transpose(bias, (0, 2, 1, 3)).astype(jnp.float32)[None]
        s = jnp.where(col_mask[None, None, :, None, :], s, -jnp.inf)
        p = jax.nn.softmax(s.reshape(B, H, GRID_W, wr * GRID_W), axis=-1).astype(v.dtype)
        return jnp.einsum('bhqn,bnhd->bqhd', p, vb.reshape(B, wr * GRID_W, H, Dh))

    o = lax.map(row_block, jnp.arange(rows))
    return jnp.transpose(o, (1, 0, 2, 3, 4)).reshape(B, T, H, Dh)

def _gated_linear_scan(q, k, v, log_f):
    B, T, H, Dk = q.shape
    Dv = v.shape[-1]
    C = HG_CHUNK
    N = T // C

    def to_chunks(a):
        return a.reshape(B, N, C, H, a.shape[-1]).transpose(1, 0, 3, 2, 4)

    causal = jnp.tril(jnp.ones((C, C), dtype=bool))

    def step(S, inp):
        qb, kb, vb, gb = inp
        A = jnp.cumsum(gb, axis=2)
        diff = A[:, :, :, None, :] - A[:, :, None, :, :]
        decay = jnp.exp(jnp.where(causal[:, :, None], diff, -jnp.inf))
        scores = jnp.sum(qb[:, :, :, None, :] * kb[:, :, None, :, :] * decay, axis=-1)
        o = jnp.einsum('bhts,bhsv->bhtv', scores, vb) + \
            jnp.einsum('bhtd,bhdv->bhtv', qb * jnp.exp(A), S)
        A_last = A[:, :, -1, :]
        S = jnp.exp(A_last)[..., None] * S + \
            jnp.einsum('bhsd,bhsv->bhdv', kb * jnp.exp(A_last[:, :, None, :] - A), vb)
        return S, o

    S0 = jnp.zeros((B, H, Dk, Dv), jnp.float32)
    _, o = lax.scan(step, S0, (to_chunks(q), to_chunks(k), to_chunks(v), to_chunks(log_f)))
    return o.transpose(1, 0, 3, 2, 4).reshape(B, T, H, Dv)

def _hgrn2_bidirectional(q, f_fwd, f_bwd, i, lb):
    q = q.astype(jnp.float32)
    i = i.astype(jnp.float32)

    def gates(fl, lbd):
        fl = fl.astype(jnp.float32)
        f = lbd + (1.0 - lbd) * jax.nn.sigmoid(fl)
        return jnp.log(f), (1.0 - lbd) * jax.nn.sigmoid(-fl)

    lf_f, k_f = gates(f_fwd, lb[0])
    lf_b, k_b = gates(f_bwd, lb[1])
    o_fwd = _gated_linear_scan(q, k_f, i, lf_f)
    flip = lambda a: jnp.flip(a, axis=1)
    o_bwd = flip(_gated_linear_scan(flip(q), flip(k_b), flip(i), flip(lf_b)))
    return o_fwd + o_bwd

def setup_inputs(seed: int = 0) -> dict:
    key = jax.random.key(seed)
    ks = jax.random.split(key, 11)
    f32 = jnp.float32
    nrm = lambda k, s: jax.random.normal(k, s, f32)
    x = nrm(ks[0], (BATCH, SEQ, D_MODEL))
    norm_pre_w = 1.0 + 0.02 * nrm(ks[1], (DEPTH, D_MODEL))
    w_in = nrm(ks[2], (DEPTH, D_MODEL, IN_COLS)) * D_MODEL ** -0.5
    b_gate = 0.02 * nrm(ks[3], (DEPTH, N_BRANCHES * D_MODEL))
    na_rel_bias = 0.1 * nrm(ks[4], (DEPTH, NA_HEADS, 2 * NA_WIN_ROWS - 1, 2 * NA_WIN_COLS - 1))
    hg_lb_logits = 0.5 * nrm(ks[5], (DEPTH + 1, 2, HG_KEY_WIDTH))
    hg_norm_w = 1.0 + 0.02 * nrm(ks[6], (DEPTH, HG_WIDTH))
    w_branch = nrm(ks[7], (DEPTH, NA_WIDTH + HG_WIDTH, D_MODEL)) * NA_WIDTH ** -0.5
    w_out = nrm(ks[8], (DEPTH, D_MODEL, D_MODEL)) * D_MODEL ** -0.5
    norm_post_w = 1.0 + 0.02 * nrm(ks[9], (DEPTH, D_MODEL))
    return {"x": x, "norm_pre_w": norm_pre_w, "w_in": w_in, "b_gate": b_gate,
            "na_rel_bias": na_rel_bias, "hg_lb_logits": hg_lb_logits, "hg_norm_w": hg_norm_w,
            "w_branch": w_branch, "w_out": w_out, "norm_post_w": norm_post_w}

def reference(x, norm_pre_w, w_in, b_gate, na_rel_bias, hg_lb_logits, hg_norm_w, w_branch, w_out, norm_post_w):
    B, T, _ = x.shape
    lb_all = jnp.cumsum(jax.nn.softmax(hg_lb_logits.astype(jnp.float32), axis=0), axis=0)
    splits = [int(s) for s in np.cumsum([NA_WIDTH] * 4 + [HG_KEY_WIDTH] * 3 + [HG_WIDTH] * 2)]
    for l in range(DEPTH):
        xn = _rmsnorm(x, norm_pre_w[l])
        h = xn @ w_in[l]
        na_q, na_k, na_v, na_z, hg_q, hg_ff, hg_fb, hg_i, hg_z, gate_pre = jnp.split(h, splits, axis=-1)

        ha = lambda a: a.reshape(B, T, NA_HEADS, NA_HEAD_DIM)
        o_a = _neighbourhood_attention(ha(na_q), ha(na_k), ha(na_v), na_rel_bias[l]).reshape(B, T, NA_WIDTH)
        o_a = o_a * jax.nn.silu(na_z)

        hk = lambda a: a.reshape(B, T, HG_HEADS, HG_KEY_DIM)
        lb = lb_all[l].reshape(2, HG_HEADS, HG_KEY_DIM)
        o_b = _hgrn2_bidirectional(hk(hg_q), hk(hg_ff), hk(hg_fb), hg_i.reshape(B, T, HG_HEADS, HG_VAL_DIM), lb)
        o_b = _rmsnorm(o_b, hg_norm_w[l].reshape(HG_HEADS, HG_VAL_DIM)).reshape(B, T, HG_WIDTH).astype(x.dtype)
        o_b = o_b * jax.nn.silu(hg_z)

        g = jax.nn.sigmoid(gate_pre + b_gate[l])
        g_a, g_b = jnp.split(g, N_BRANCHES, axis=-1)
        y = g_a * (o_a @ w_branch[l, :NA_WIDTH]) + g_b * (o_b @ w_branch[l, NA_WIDTH:])
        x = x + _rmsnorm(y @ w_out[l], norm_post_w[l])
    return x


_drawn_inputs = setup_inputs


def setup_inputs(seed=0):
    import zlib

    import numpy as np

    out = dict(_drawn_inputs(seed))
    spreads = {}
    factors = {'b_gate': 8.0, 'na_rel_bias': 12.269, 'hg_norm_w': 11.446, 'norm_post_w': 11.275}
    for name, (base, spread) in spreads.items():
        noise = np.random.default_rng([zlib.crc32(name.encode()), seed]).standard_normal(out[name].shape)
        drawn = base * np.exp(spread * noise) if base else spread * noise
        out[name] = __import__('jax').numpy.asarray(drawn.astype(out[name].dtype))
    for name, factor in factors.items():
        out[name] = (out[name] * factor).astype(out[name].dtype)
    return out
```

```python
from contextlib import ExitStack

import concourse.bass as bass
from concourse import mybir

ALU = mybir.AluOpType
ACT = mybir.ActivationFunctionType
AX = mybir.AxisListType
F32 = mybir.dt.float32
F32R = mybir.dt.float32r
U32 = mybir.dt.uint32

P = 128
T = 256
D = 2048
KT = D // P
NG = 8
GRID_W = 64
ROWS = T // GRID_W
HEAD = 64
WIN_C = 16
BIAS_R, BIAS_C = 15, 31
EPS = 1e-6
NEG = -1e30
IN_SLOTS = 12
TAIL = 8
N_IN = NG * IN_SLOTS + TAIL
N_BR = D // P
N_OUT = 16
RAW = 4
HALVES = 4
LEVELS = 8
NSLOT_Q, NSLOT_K, NSLOT_V, NSLOT_Z, NSLOT_F, NSLOT_B, NSLOT_HQ, NSLOT_I, NSLOT_HZ = range(9)
COL_TILE = [0, 8, 16, 24, 40, 48, 32, 56, 64]
GATE_TILE = 72


class Steps:

    def __init__(self, sem, per_group):
        self.sem, self.per_group, self.base, self.k = sem, per_group, 0, 0

    def begin(self, g):
        self.base, self.k = g * self.per_group, 0

    def resume(self, g):
        self.base = g * self.per_group

    def done(self, instruction):
        instruction.then_inc(self.sem, 1)
        self.k += 1

    def settle(self, engine, but=0):
        engine.wait_ge(self.sem, self.base + (self.k - but))

    def end(self):
        assert self.k == self.per_group, (self.k, self.per_group)


def encoder_layer(nc, x, norm_pre_w, w_in, b_gate, na_rel_bias, hg_lb_logits, hg_norm_w, w_branch,
                  w_out, norm_post_w, out):
    w_in_v = w_in[0].rearrange("(k p) n -> p k n", p=P)
    w_branch_v = w_branch[0].rearrange("(k p) n -> p k n", p=P)
    w_out_v = w_out[0].rearrange("(k p) n -> p k n", p=P)

    with ExitStack() as ctx:
        def sb(name, shape, dt=F32):
            return ctx.enter_context(nc.sbuf_tensor(name, shape, dt))

        def sem(name):
            return ctx.enter_context(nc.semaphore(name))

        act_hl = sb("act_hl", [P, KT, 2 * T], F32R)
        branch_hl = sb("branch_hl", [P, 2 * NG, 2 * T], F32R)
        raw = sb("raw", [P, RAW, 2 * 1024])
        w_hi = sb("w_hi", [P, HALVES, 1024], F32R)
        w_lo = sb("w_lo", [P, HALVES, 1024], F32R)
        big = sb("big", [P, 32, T])
        gates = big
        x_tok = big[:, 0:16, :].rearrange("p (t a) c -> p t (a c)", t=2)
        xs_tok = big[:, 16:32, :].rearrange("p (t a) c -> p t (a c)", t=2)
        o_tok = xs_tok
        bias_t = sb("bias_t", [P, 2, 6 * GRID_W])
        part = sb("part", [P, 2, T])
        na = sb("na", [P, 5, T])
        na_q, na_k, na_v, na_z, na_th = (na[:, i, :] for i in range(5))
        v_tok = sb("v_tok", [P, 2, P])
        wide = sb("wide", [P, 4, 2 * T])
        prob, prob_t = wide[:, 0:2, :], wide[:, 2:4, :]
        hg = sb("hg", [P, 14, T])
        pre_f, suf_f, suf_b, pre_b, hq, key_f, key_b, key_s, i_feat, hz, hth, o_h, o_sq, rst_rows = (
            hg[:, i, :] for i in range(14))
        q_dec = sb("q_dec", [P, 2, T])
        k_dec = sb("k_dec", [P, 2, T])
        scores_t = sb("scores_t", [P, 4 * P])
        i_tok = sb("i_tok", [P, 2, P])
        block = sb("block", [P, 7, P])
        ones = sb("ones", [P, P])
        win = sb("win", [P, 2, GRID_W])
        vec_rows = sb("vec_rows", [88, P])
        vec = sb("vec", [P, 88])
        small = sb("small", [P, 128])
        lb0, lb1, lb_m, lb_r = (small[:, 16 * i:16 * i + 16] for i in range(4))
        half_open = small[:, 64:80]
        half_shut = small[:, 80:96]
        mid = small[:, 96:112]
        half_hgw = small[:, 112:120]
        small2 = sb("small2", [P, 64])
        half_bg = small2[:, 0:32]
        ssq = small2[:, 32:40]
        ssum, msq, rstd = small2[:, 40:42], small2[:, 42:44], small2[:, 44:46]
        nmax, rsum, rinv = small2[:, 46:50], small2[:, 50:54], small2[:, 54:58]
        neg_half = small2[:, 58:59]
        hg_ms, hg_rst = small2[:, 59:61], small2[:, 61:63]
        y_sums = (o_sq, o_h)
        post_w = wide[:, :, :].rearrange("p a b -> p (a b)")

        bank = [ctx.enter_context(nc.psum_tensor(f"bank{i}", [P, 512], F32)) for i in range(8)]
        ps_proj, ps_lvl = bank[0:2], bank[2:4]
        ps_s, ps_pt, ps_o, ps_tr = bank[4:8]
        out_bank = [bank[4:6], bank[6:8], bank[0:2], bank[2:4]]

        raw_landed = [sem(f"raw_landed{i}") for i in range(RAW)]
        hi_ready = sem("hi_ready")
        lo_ready = sem("lo_ready")
        half_used = sem("half_used")
        part_ready = sem("part_ready")
        tile_out = sem("tile_out")
        vec_landed, x0_landed, x1_landed = sem("vec_landed"), sem("x0_landed"), sem("x1_landed")
        const_step, ones_ready, win_ready = sem("const_step"), sem("ones_ready"), sem("win_ready")
        masks_ready = sem("masks_ready")
        vec_turned, vec_ready = sem("vec_turned"), sem("vec_ready")
        setup_step = sem("setup_step")
        ss0_ready, msq_ready, rstd_ready = sem("ss0_ready"), sem("msq_ready"), sem("rstd_ready")
        xs_ready, xt_done, xhi_ready, xn_ready = (
            sem("xs_ready"), sem("xt_done"), sem("xhi_ready"), sem("xn_ready"))
        lbm_ready, lbe_ready = sem("lbm_ready"), sem("lbe_ready")
        bias_landed, bias_ready = sem("bias_landed"), sem("bias_ready")
        s_done, s_taken = sem("s_done"), sem("s_taken")
        max_ready, exp_ready, prob_ready = sem("max_ready"), sem("exp_ready"), sem("prob_ready")
        tr_done, tr_taken = sem("tr_done"), sem("tr_taken")
        pt_done, pt_taken = sem("pt_done"), sem("pt_taken")
        pv_done, nz_tanh = sem("pv_done"), sem("nz_tanh")
        oa_ready, oa_hi, oa_lo = sem("oa_ready"), sem("oa_hi"), sem("oa_lo")
        na_step = sem("na_step")
        f_tanh, b_tanh, hz_tanh = sem("f_tanh"), sem("b_tanh"), sem("hz_tanh")
        dec_ready, lvl_done, lvl_taken = sem("dec_ready"), sem("lvl_done"), sem("lvl_taken")
        hg_out, osq_ready, ms_done = sem("hg_out"), sem("osq_ready"), sem("ms_done")
        ms_ready, rst_ready, rst_spread, rst_turned = (
            sem("ms_ready"), sem("rst_ready"), sem("rst_spread"), sem("rst_turned"))
        ob_ready, ob_hi, ob_lo = sem("ob_ready"), sem("ob_hi"), sem("ob_lo")
        hg_step, ob_step = sem("hg_step"), sem("ob_step")
        gate_ready = sem("gate_ready")
        y_sum, y_hi, y_ready, y_step = sem("y_sum"), sem("y_hi"), sem("y_ready"), sem("y_step")
        tail_landed, block_sq, out_taken = sem("tail_landed"), sem("block_sq"), sem("out_taken")
        fin_step, msq2_ready, rstd2_ready = sem("fin_step"), sem("msq2_ready"), sem("rstd2_ready")
        out_ready, out_stored = sem("out_ready"), sem("out_stored")

        def wait(engine, semaphore, value):
            if isinstance(value, int) and value <= 0:
                return
            engine.wait_ge(semaphore, value)

        def tile_no(g, s):
            return g * IN_SLOTS + s

        def raw_count(n4, r):
            return n4 * 16 + 16

        def at(ap, i):
            if isinstance(i, int):
                return ap[:, i]
            return ap[:, bass.ds(i, 1)].rearrange("p a b -> p (a b)")

        def column(ap, i):
            return ap[:, i:i + 1] if isinstance(i, int) else ap[:, bass.ds(i, 1)]

        def pairs(ap, half):
            return ap.rearrange("p (n two h) -> p n two h", two=2, h=half)

        def both_tiles(ap):
            return bass.AP(ap.tensor, ap.offset, [list(ap.ap[0]), [3 * P, 2], [1, P]])

        blk = ctx.enter_context(nc.Block())

        @blk.sync
        def _(sp):
            def load(r, src, n):
                wait(sp, lo_ready, n * 2 - 2 * RAW + 2)
                dst = raw[:, r, :]
                k = src.shape[1]
                sp.dma_start(dst.rearrange("p (k c) -> p k c", k=k), src).then_inc(raw_landed[r], 16)

            def load_bias(g):
                wait(sp, s_taken, g * 2)
                for parity in range(2):
                    for a in range(2):
                        src = bass.AP(na_rel_bias.tensor,
                                      (g * 2 + a) * (BIAS_R * BIAS_C) + (5 - parity) * BIAS_C + 15 - (GRID_W - 1),
                                      [[1, GRID_W], [BIAS_C, 6], [1, GRID_W]])
                        dst = bias_t[GRID_W * parity:GRID_W * (parity + 1), a, :]
                        sp.dma_start(dst.rearrange("p (m c) -> p m c", m=6), src).then_inc(bias_landed, 16)

            def group(g):
                for s in range(IN_SLOTS):
                    if s == 1:
                        load_bias(g)
                    col = g + COL_TILE[s] if s < 9 else g * 3 + (GATE_TILE + s - 9)
                    cols = slice(col * P, col * P + P) if isinstance(g, int) else bass.ds(col * P, P)
                    load(s % RAW, w_in_v[:, :, cols], tile_no(g, s))

            sp.dma_start(x_tok[:, 0, :], x[0, 0:P, :]).then_inc(x0_landed, 16)
            sp.dma_start(x_tok[:, 1, :], x[0, P:T, :]).then_inc(x1_landed, 16)
            group(0)
            with sp.Fori(1, NG) as g:
                group(g)
            for t in range(TAIL):
                col = GATE_TILE + 3 * NG + t
                load(t % RAW, w_in_v[:, :, col * P:col * P + P], tile_no(NG, t))
            with sp.Fori(0, N_BR // RAW) as jj:
                for r in range(RAW):
                    load(r, w_branch_v[:, :, bass.ds(jj * (RAW * P) + r * P, P)], jj * RAW + (N_IN + r))
            with sp.Fori(0, 4) as c:
                for r in range(4):
                    load(r, w_out_v[:, 4 * r:4 * r + 4, bass.ds(c * 512, 512)], c * RAW + (N_IN + N_BR + r))
            for i in range(8):
                t, c = i // 4, i % 4
                sp.wait_ge(out_ready, i + 1)
                sp.dma_start(out[0, t * P:(t + 1) * P, c * 512:(c + 1) * 512],
                             o_tok[:, t, c * 512:(c + 1) * 512]).then_inc(out_stored, 16)
            sp.wait_ge(out_stored, 8 * 16)

        @blk.gpsimd
        def _(pool):
            nc.gpsimd.memset(ones[:, :], 1.0).then_inc(const_step, 1)
            nc.gpsimd.memset(win[:, :, :], 0.0).then_inc(const_step, 1)
            nc.gpsimd.memset(neg_half, -0.5).then_inc(const_step, 1)
            pool.wait_ge(const_step, 1)
            steps = 3
            for i in range(7):
                if i == 1:
                    pool.wait_ge(msq_ready, 1)
                    nc.gpsimd.tensor_tensor(rstd, msq, neg_half.to_broadcast([P, 2]),
                                            ALU.pow).then_inc(rstd_ready, 1)
                n = 1 << i
                v = block[:, i, :].rearrange("p (b w) -> p b w", w=n)
                src = ones[:, :].rearrange("p (b w) -> p b w", w=n)
                nc.gpsimd.affine_select(out=v, in_=src, compare_op=ALU.is_ge, fill=0.0, base=0,
                                        pattern=[[-n, P // n], [0, n]], channel_multiplier=1).then_inc(const_step, 1)
                steps += 1
                pool.wait_ge(const_step, steps)
                nc.gpsimd.affine_select(out=v, in_=v, compare_op=ALU.is_ge, fill=0.0, base=n - 1,
                                        pattern=[[n, P // n], [0, n]], channel_multiplier=-1).then_inc(const_step, 1)
                steps += 1
            pool.wait_ge(const_step, steps)
            for sel in ((win[:, :, 0:GRID_W - WIN_C], 1, -(GRID_W - 1 - WIN_C // 2)),
                        (win[:, :, WIN_C:GRID_W], -1, GRID_W - 1 + WIN_C // 2 - 1 - WIN_C)):
                v, sign, base = sel
                nc.gpsimd.affine_select(out=v, in_=v, compare_op=ALU.is_ge, fill=NEG, base=base,
                                        pattern=[[-GRID_W * sign, 2], [sign, GRID_W - WIN_C]],
                                        channel_multiplier=sign).then_inc(const_step, 1)
                steps += 1
                pool.wait_ge(const_step, steps)
            for base, step, mult in ((0, -GRID_W, 1), (GRID_W - 1, GRID_W, -1)):
                nc.gpsimd.affine_select(out=win[:, :, :], in_=win[:, :, :], compare_op=ALU.is_ge, fill=0.0,
                                        base=base, pattern=[[step, 2], [0, GRID_W]],
                                        channel_multiplier=mult).then_inc(const_step, 1)
                steps += 1
                pool.wait_ge(const_step, steps)
            nc.gpsimd.tensor_tensor(win[:, 0, :], win[:, 0, :], win[:, 1, :], ALU.add).then_inc(win_ready, 1)
            pool.wait_ge(win_ready, 1)

            def mask_bias(g):
                pool.wait_ge(bias_landed, g * 64 + 64)
                v = bias_t[:, :, :].rearrange("p a (m c) -> p (a m) c", c=GRID_W)
                w = win[:, 0:1, :].to_broadcast([P, 12, GRID_W])
                nc.gpsimd.tensor_tensor(v, v, w, ALU.add).then_inc(bias_ready, 1)

            def power(g):
                pool.wait_ge(ms_ready, g + 1)
                nc.gpsimd.tensor_tensor(hg_rst, hg_ms, neg_half.to_broadcast([P, 2]), ALU.pow).then_inc(rst_ready, 1)

            mask_bias(0)
            with pool.Fori(1, NG) as g:
                mask_bias(g)
                power(g - 1)
            power(NG - 1)
            pool.wait_ge(msq2_ready, 1)
            nc.gpsimd.tensor_tensor(rstd, msq, neg_half.to_broadcast([P, 2]), ALU.pow).then_inc(rstd2_ready, 1)

        @blk.scalar
        def _(act):
            def split_hi(n, r, n4, h):
                if h == 0:
                    act.wait_ge(raw_landed[r], raw_count(n4, r))
                wait(act, half_used, n * 2 + h - HALVES + 1)
                nc.scalar.activation(w_hi[:, (2 * r + h) % HALVES, :], raw[:, r, 1024 * h:1024 * (h + 1)],
                                     ACT.Copy).then_inc(hi_ready, 1)

            def split_next(n, n4, r):
                r1, c1 = (r + 1) % RAW, n4 + (r + 1) // RAW
                split_hi(n + 1, r1, c1, 0)
                split_hi(n + 1, r1, c1, 1)

            def take_part(n, b):
                act.wait_ge(half_used, n * 2 + 2)
                nc.scalar.activation(part[:, b, :], ps_proj[b][:, T:2 * T], ACT.Copy).then_inc(part_ready, 1)

            def gate_tanh(i, n):
                act.wait_ge(tile_out, n + 1)
                v = at(gates, i)
                nc.scalar.activation(v, v, ACT.Tanh, scale=0.5, bias=column(half_bg, i)).then_inc(gate_ready, 1)

            def tanh_half(v, n, semaphore):
                act.wait_ge(tile_out, n + 1)
                nc.scalar.activation(v[0], v[1], ACT.Tanh, scale=0.5).then_inc(semaphore, 1)

            def exp_head(g, a):
                act.wait_ge(max_ready, g * 2 + a + 1)
                for u in range(2):
                    v = prob[:, a, u * T:(u + 1) * T]
                    i = 2 * a + u
                    nc.scalar.activation(v, v, ACT.Exp, bias=nmax[:, i:i + 1],
                                         accum_out=rsum[:, i:i + 1]).then_inc(exp_ready, 1)

            def take_prob_t(g, a):
                act.wait_ge(pt_done, g * 2 + a + 1)
                nc.scalar.activation(prob_t[:, a, :], ps_pt[:, :], ACT.Copy).then_inc(pt_taken, 1)

            def attention(g, s):
                n = tile_no(g, s)
                if s == 3:
                    exp_head(g, 0)
                if s == 4:
                    act.wait_ge(tr_done, g * 2 + 1)
                    nc.scalar.activation(v_tok[:, :, :].rearrange("p a b -> p (a b)"), ps_tr[:, 0:T],
                                         ACT.Copy).then_inc(tr_taken, 1)
                    tanh_half((na_th, na_z), n - 1, nz_tanh)
                    exp_head(g, 1)
                if s == 5:
                    tanh_half((pre_f, pre_f), n - 1, f_tanh)
                if s == 6:
                    take_prob_t(g, 0)
                    tanh_half((suf_b, suf_b), n - 1, b_tanh)
                if s == 7:
                    take_prob_t(g, 1)
                if s == 9:
                    act.wait_ge(tr_done, g * 2 + 2)
                    nc.scalar.activation(i_tok[:, :, :].rearrange("p a b -> p (a b)"), ps_tr[:, 0:T],
                                         ACT.Copy).then_inc(tr_taken, 1)
                    tanh_half((hth, hz), n - 1, hz_tanh)
                    act.wait_ge(oa_ready, g + 1)
                    nc.scalar.activation(at(branch_hl, g)[:, 0:T], na_th, ACT.Copy).then_inc(oa_hi, 1)
                if s == 10:
                    gate_tanh(g * 3, n - 1)
                if s == 11:
                    gate_tanh(g * 3 + 1, n - 1)

            def out_square(g):
                act.wait_ge(hg_out, g + 1)
                nc.scalar.activation(o_h, ps_lvl[0][:, 0:T], ACT.Copy)
                nc.scalar.activation(o_sq, ps_lvl[0][:, 0:T], ACT.Square).then_inc(osq_ready, 1)

            def hgrn_hi(g):
                act.wait_ge(ob_ready, g + 1)
                nc.scalar.activation(at(branch_hl, g + NG)[:, 0:T], o_h, ACT.Copy).then_inc(ob_hi, 1)

            def previous(g, s):
                if s == 0:
                    gate_tanh((g - 1) * 3 + 2, tile_no(g, -1))
                if s == 6:
                    out_square(g - 1)
                if s == 9:
                    hgrn_hi(g - 1)

            def group(g, first):
                for s in range(IN_SLOTS):
                    n, n4, r = tile_no(g, s), g * 3 + s // RAW, s % RAW
                    split_next(n, n4, r)
                    if not first:
                        previous(g, s)
                    attention(g, s)
                    take_part(n, s % 2)

            rows = ((0, hg_lb_logits.rearrange("l d (h c) -> (l d h) c", c=P)),
                    (32, b_gate.rearrange("o (h c) -> (o h) c", c=P)),
                    (64, norm_pre_w.rearrange("o (h c) -> (o h) c", c=P)),
                    (80, hg_norm_w.rearrange("o (h c) -> (o h) c", c=P)))
            for r0, src in rows:
                act.dma_start(vec_rows[r0:r0 + src.shape[0], :], src).then_inc(vec_landed, 16)
            act.wait_ge(x0_landed, 16)
            nc.scalar.activation(xs_tok[:, 0, :], x_tok[:, 0, :], ACT.Square,
                                 accum_out=ssq[:, 0:1]).then_inc(ss0_ready, 1)
            act.wait_ge(x1_landed, 16)
            nc.scalar.activation(xs_tok[:, 1, 0:D // 2], x_tok[:, 1, 0:D // 2], ACT.Square,
                                 accum_out=ssq[:, 2:3]).then_inc(ss0_ready, 1)
            split_hi(0, 0, 0, 0)
            for k in range(KT):
                if k == 8:
                    split_hi(0, 0, 0, 1)
                act.wait_ge(xt_done, k // 2 + 1)
                nc.scalar.activation(act_hl[:, k, 0:T], bank[k // 2][:, (k % 2) * T:(k % 2 + 1) * T], ACT.Copy,
                                     scale=vec[:, 64 + k:65 + k]).then_inc(xhi_ready, 1)

            act.wait_ge(lbm_ready, 1)
            nc.scalar.activation(lb0, lb0, ACT.Exp)
            nc.scalar.activation(lb1, lb1, ACT.Exp).then_inc(lbe_ready, 1)
            group(0, True)
            with act.Fori(1, NG) as g:
                group(g, False)
            for t in range(TAIL):
                n = tile_no(NG, t)
                split_next(n, n // RAW, n % RAW)
                if t > 0:
                    gate_tanh(3 * NG + t - 1, n - 1)
                previous(NG, t)
                take_part(n, t % 2)
            gate_tanh(3 * NG + TAIL - 1, tile_no(NG, TAIL - 1))
            hgrn_hi(NG - 1)

            def take_branch(n, b, j):
                act.wait_ge(half_used, n * 2 + 1)
                wait(act, y_sum, j)
                nc.scalar.activation(part[:, 0, :], ps_proj[b][:, T:2 * T], ACT.Copy).then_inc(part_ready, 1)
                act.wait_ge(half_used, n * 2 + 2)
                nc.scalar.activation(part[:, 1, :], ps_lvl[b][:, T:2 * T], ACT.Copy).then_inc(part_ready, 1)

            def split_y(j, b):
                act.wait_ge(y_sum, j + 1)
                nc.scalar.activation(at(act_hl, j)[:, 0:T], y_sums[b], ACT.Copy,
                                     scale=0.5).then_inc(y_hi, 1)

            act.wait_ge(tile_out, N_IN)
            act.wait_ge(pv_done, NG)
            act.dma_start(post_w, norm_post_w.partition_broadcast(P)).then_inc(tail_landed, 16)
            for r in range(RAW):
                split_next(N_IN + r, N_IN // RAW, r)
                if r:
                    split_y(r - 1, (r - 1) % 2)
                take_branch(N_IN + r, r % 2, r)
            with act.Fori(1, N_BR // RAW) as jj:
                for r in range(RAW):
                    n = jj * RAW + (N_IN + r)
                    split_next(n, jj + N_IN // RAW, r)
                    split_y(jj * RAW + (r - 1), (r - 1) % 2)
                    take_branch(n, r % 2, jj * RAW + r)
            split_y(N_BR - 1, 1)
            for t in range(2):
                act.dma_start(x_tok[:, t, :], x[0, t * P:(t + 1) * P, :]).then_inc(tail_landed, 16)
            for q in range(N_OUT):
                n = N_IN + N_BR + q
                if q < N_OUT - 1:
                    split_next(n, n // RAW, q % RAW)
                if q % 4 == 3:
                    c = q // 4
                    act.wait_ge(half_used, n * 2 + 2)
                    for t in range(2):
                        b = out_bank[c][t]
                        nc.scalar.activation(hg[:, 0:2, :].rearrange("p a b -> p (a b)"), b[:, :], ACT.Square,
                                             accum_out=ssq[:, 4 * t + c:4 * t + c + 1]).then_inc(block_sq, 1)
                        act.wait_ge(block_sq, 2 * c + t + 1)

        @blk.vector
        def _(dve):
            na_s, hg_s, ob_s = Steps(na_step, 3), Steps(hg_step, 2 * 2 + 1 + 1 + 4 * (LEVELS - 1)), Steps(ob_step, 2)

            def split_lo(n, r, h):
                dve.wait_ge(hi_ready, n * 2 + h + 1)
                i = (2 * r + h) % HALVES
                nc.vector.tensor_tensor(w_lo[:, i, :], raw[:, r, 1024 * h:1024 * (h + 1)],
                                        w_hi[:, i, :].bitcast(F32), ALU.subtract).then_inc(lo_ready, 1)

            def split_next(n, r):
                split_lo(n + 1, (r + 1) % RAW, 0)
                split_lo(n + 1, (r + 1) % RAW, 1)

            def take_tile(n, b, dst):
                dve.wait_ge(part_ready, n + 1)
                if dst is na_q:
                    dst = na_q.rearrange("p (r c) -> p r c", c=GRID_W)[:, :, ::-1]
                    src = ps_proj[b][:, 0:T].rearrange("p (r c) -> p r c", c=GRID_W)
                    prt = part[:, b, :].rearrange("p (r c) -> p r c", c=GRID_W)
                else:
                    src, prt = ps_proj[b][:, 0:T], part[:, b, :]
                nc.vector.tensor_tensor(dst, src, prt, ALU.add).then_inc(tile_out, 1)

            def scores_and_max(g, a):
                dve.wait_ge(s_done, g * 2 + a + 1)
                if a == 0:
                    dve.wait_ge(bias_ready, g + 1)
                bias = bass.AP(bias_t[:, :, :].tensor, a * 6 * GRID_W, [[12 * GRID_W, P], [2 * GRID_W, 2], [1, T]])
                pv = prob[:, a, :].rearrange("p (u k) -> p u k", u=2)
                nc.vector.scalar_tensor_tensor(out=pv, in0=ps_s[:, :].rearrange("p (u k) -> p u k", u=2),
                                               scalar=HEAD ** -0.5, in1=bias, op0=ALU.mult,
                                               op1=ALU.add).then_inc(s_taken, 1)
                dve.wait_ge(s_taken, g * 2 + a + 1)
                nc.vector.tensor_reduce(nmax[:, 2 * a:2 * a + 2], pv, AX.X, ALU.max,
                                        negate=True).then_inc(max_ready, 1)

            def normalise(g, a):
                dve.wait_ge(exp_ready, g * 4 + 2 * a + 2)
                na_s.done(nc.vector.reciprocal(rinv[:, 2 * a:2 * a + 2], rsum[:, 2 * a:2 * a + 2]))
                na_s.settle(dve)
                for u in range(2):
                    v = prob[:, a, u * T:(u + 1) * T]
                    ins = nc.vector.tensor_scalar(v, v, rinv[:, 2 * a + u:2 * a + u + 1], None, ALU.mult)
                ins.then_inc(prob_ready, 1)

            def gate_constants(v, key, semaphore, g, direction):
                dve.wait_ge(semaphore, g + 1)
                i = g + 8 * direction
                hg_s.done(nc.vector.tensor_scalar(key, v, column(half_shut, i), column(half_open, i),
                                                  ALU.mult, ALU.add))
                hg_s.done(nc.vector.tensor_scalar(v, v, column(half_open, i), column(mid, i), ALU.mult, ALU.add))

            def grow(half):
                def bc(ap, side, pos):
                    return pairs(ap, half)[:, :, side, pos:pos + 1].to_broadcast([P, T // (2 * half), half])
                for i, (dst, side, src) in enumerate((
                        (suf_f, 0, bc(pre_f, 1, half - 1)), (pre_b, 1, bc(suf_b, 0, 0)),
                        (pre_f, 1, bc(pre_f, 0, half - 1)), (suf_b, 0, bc(suf_b, 1, 0)))):
                    if i >= 2:
                        hg_s.settle(dve, but=1)
                    d = pairs(dst, half)[:, :, side, :]
                    hg_s.done(nc.vector.tensor_tensor(d, d, src, ALU.mult))

            def decayed(g, level):
                half, b = 1 << level, level % 2
                hg_s.settle(dve)
                if level > 0:
                    dve.wait_ge(dec_ready, g * 8 + level)
                    grow(half // 2)
                    hg_s.settle(dve)
                for dst, side, v, w in ((q_dec, 1, hq, pre_f), (q_dec, 0, hq, suf_b),
                                        (k_dec, 0, key_f, suf_f), (k_dec, 1, key_b, pre_b)):
                    ins = nc.vector.tensor_tensor(*(pairs(i, half)[:, :, side, :] for i in (dst[:, b, :], v, w)),
                                                  ALU.mult)
                ins.then_inc(dec_ready, 1)

            def take_and_decay(g, level):
                dve.wait_ge(lvl_done, g * 8 + level + 1)
                src = ps_lvl[level % 2]
                if level == LEVELS - 1:
                    nc.vector.tensor_copy(scores_t[:, P:3 * P], src[:, 0:T]).then_inc(lvl_taken, 1)
                    hg_s.end()
                    return
                data = src[:, 0:T].rearrange("p (a t) -> p a t", a=2)
                if level == 0:
                    hg_s.done(nc.vector.tensor_copy(both_tiles(scores_t[:, :]), data))
                    data = src[:, T:2 * T].rearrange("p (a t) -> p a t", a=2)
                else:
                    dve.wait_ge(lvl_taken, g * 8 + level)
                decayed(g, level + 1)
                mask = block[:, level:level + 1, :].bitcast(U32).to_broadcast([P, 2, P])
                nc.vector.copy_predicated(both_tiles(scores_t[:, :]), mask, data).then_inc(lvl_taken, 1)

            def attention(g, s):
                if s == 3:
                    na_s.begin(g)
                    scores_and_max(g, 0)
                if s == 4:
                    scores_and_max(g, 1)
                    normalise(g, 0)
                if s == 5:
                    normalise(g, 1)
                if s == 6:
                    hg_s.begin(g)
                    gate_constants(pre_f, key_f, f_tanh, g, 0)
                if s == 7:
                    gate_constants(suf_b, key_b, b_tanh, g, 1)
                    nc.vector.memset(suf_f, 1.0)
                    nc.vector.memset(pre_b, 1.0)
                    hg_s.settle(dve)
                    hg_s.done(nc.vector.tensor_tensor(key_s, key_f, key_b, ALU.add))
                if s == 8:
                    dve.wait_ge(nz_tanh, g + 1)
                    na_s.done(nc.vector.scalar_tensor_tensor(out=na_th, in0=na_th, scalar=1.0, in1=na_z,
                                                             op0=ALU.add, op1=ALU.mult))
                    dve.wait_ge(pv_done, g + 1)
                    na_s.settle(dve)
                    v = na_th.rearrange("p (r c) -> p r c", c=GRID_W)
                    o = ps_o[:, 0:T].rearrange("p (r c) -> p r c", c=GRID_W)[:, :, ::-1]
                    nc.vector.scalar_tensor_tensor(out=v, in0=v, scalar=0.5, in1=o, op0=ALU.mult,
                                                   op1=ALU.mult).then_inc(oa_ready, 1)
                    dve.wait_ge(tile_out, tile_no(g, NSLOT_HQ + 1))
                    decayed(g, 0)
                if s >= 9:
                    take_and_decay(g, s - 9)
                if s == 10:
                    dve.wait_ge(oa_hi, g + 1)
                    nc.vector.tensor_tensor(at(branch_hl, g)[:, T:2 * T], na_th,
                                            at(branch_hl, g)[:, 0:T].bitcast(F32), ALU.subtract).then_inc(oa_lo, 1)

            def mean_square(g):
                dve.wait_ge(ms_done, g + 1)
                nc.vector.tensor_scalar(hg_ms, ps_lvl[1][:, 0:2], 1.0 / P, EPS, ALU.mult, ALU.add).then_inc(ms_ready, 1)
                dve.wait_ge(rst_ready, g + 1)
                for i in range(2):
                    ins = nc.vector.tensor_scalar(rst_rows[:, i * P:(i + 1) * P], ones[:, :], hg_rst[:, i:i + 1], None,
                                                  ALU.mult)
                ins.then_inc(rst_spread, 1)

            def hgrn_out(g):
                ob_s.begin(g)
                dve.wait_ge(hz_tanh, g + 1)
                ob_s.done(nc.vector.scalar_tensor_tensor(out=hth, in0=hth, scalar=1.0, in1=hz, op0=ALU.add,
                                                         op1=ALU.mult))
                dve.wait_ge(rst_turned, g + 1)
                ob_s.done(nc.vector.scalar_tensor_tensor(out=o_h, in0=o_h, scalar=column(half_hgw, g),
                                                         in1=ps_lvl[1][:, 0:T],
                                                         op0=ALU.mult, op1=ALU.mult))
                ob_s.settle(dve)
                ob_s.end()
                nc.vector.tensor_tensor(o_h, o_h, hth, ALU.mult).then_inc(ob_ready, 1)

            def hgrn_lo(g):
                dve.wait_ge(ob_hi, g + 1)
                nc.vector.tensor_tensor(at(branch_hl, g + NG)[:, T:2 * T], o_h,
                                        at(branch_hl, g + NG)[:, 0:T].bitcast(F32), ALU.subtract).then_inc(ob_lo, 1)

            def previous(g, s):
                if s == 0:
                    hg_s.resume(g - 1)
                if s < 5:
                    take_and_decay(g - 1, 3 + s)
                if s == 7:
                    mean_square(g - 1)
                if s == 8:
                    hgrn_out(g - 1)
                if s == 10:
                    hgrn_lo(g - 1)

            tile_dst = [na_q, na_k, na_v, na_z, pre_f, suf_b, hq, i_feat, hz]

            def group(g, first):
                for s in range(IN_SLOTS):
                    split_next(tile_no(g, s), s % RAW)
                    if not first:
                        previous(g, s)
                    attention(g, s)
                    dst = tile_dst[s] if s < 9 else at(gates, g * 3 + (s - 9))
                    take_tile(tile_no(g, s), s % 2, dst)

            k = 0

            def link(ins):
                nonlocal k
                ins.then_inc(setup_step, 1)
                k += 1
                dve.wait_ge(setup_step, k)

            dve.wait_ge(vec_turned, 1)
            link(nc.vector.tensor_copy(vec[:, :], ps_tr[:, 0:88]))
            nc.vector.tensor_tensor(lb_m, vec[:, 0:16], vec[:, 16:32], ALU.max).then_inc(vec_ready, 1)
            nc.vector.memset(ssq[:, 1:2], 0.0)
            dve.wait_ge(x1_landed, 16)
            link(nc.vector.tensor_tensor_reduce(out=xs_tok[:, 1, D // 2:D], in0=x_tok[:, 1, D // 2:D],
                                                in1=x_tok[:, 1, D // 2:D], scale=1.0, scalar=0.0, op0=ALU.mult,
                                                op1=ALU.add, accum_out=ssq[:, 3:4]))
            dve.wait_ge(ss0_ready, 2)
            link(nc.vector.tensor_reduce(ssum, ssq[:, 0:4].rearrange("p (t c) -> p t c", t=2), AX.X, ALU.add))
            nc.vector.tensor_scalar(msq, ssum, 1.0 / D, EPS, ALU.mult, ALU.add).then_inc(msq_ready, 1)
            dve.wait_ge(rstd_ready, 1)
            for t in range(2):
                nc.vector.tensor_scalar(xs_tok[:, t, :], x_tok[:, t, :], rstd[:, t:t + 1], None,
                                        ALU.mult).then_inc(xs_ready, 1)
            for i in range(KT):
                if i == 0:
                    split_lo(0, 0, 0)
                if i == 8:
                    split_lo(0, 0, 1)
                if i % 2 == 0:
                    dve.wait_ge(xhi_ready, i + 2)
                nc.vector.scalar_tensor_tensor(out=act_hl[:, i, T:2 * T],
                                               in0=bank[i // 2][:, (i % 2) * T:(i % 2 + 1) * T],
                                               scalar=vec[:, 64 + i:65 + i], in1=act_hl[:, i, 0:T].bitcast(F32),
                                               op0=ALU.mult, op1=ALU.subtract).then_inc(xn_ready, 1)
            dve.wait_ge(vec_ready, 1)
            nc.vector.tensor_tensor(lb0, vec[:, 0:16], lb_m, ALU.subtract)
            nc.vector.tensor_tensor(lb1, vec[:, 16:32], lb_m, ALU.subtract).then_inc(lbm_ready, 1)
            nc.vector.tensor_scalar(half_bg, vec[:, 32:64], 0.5, None, ALU.mult)
            nc.vector.tensor_scalar(half_hgw, vec[:, 80:88], 0.5, None, ALU.mult).then_inc(vec_ready, 1)
            dve.wait_ge(lbe_ready, 1)
            link(nc.vector.tensor_tensor(lb_r, lb0, lb1, ALU.add))
            link(nc.vector.reciprocal(lb_r, lb_r))
            link(nc.vector.tensor_tensor(lb0, lb0, lb_r, ALU.mult))
            link(nc.vector.tensor_tensor(lb1, lb1, lb_r, ALU.mult))
            link(nc.vector.tensor_scalar(half_open, lb1, 0.5, None, ALU.mult))
            nc.vector.tensor_scalar(half_shut, lb1, -0.5, None, ALU.mult)
            link(nc.vector.tensor_tensor(mid, lb0, half_open, ALU.add))
            dve.wait_ge(const_step, 3 + 14)
            for level in range(1, 7):
                same = block[:, level, :]
                if level < 6:
                    ins = nc.vector.tensor_tensor(same, block[:, level + 1, :], same, ALU.subtract)
                else:
                    ins = nc.vector.tensor_scalar(same, same, -1.0, 1.0, ALU.mult, ALU.add)
                ins.then_inc(masks_ready, 1)

            group(0, True)
            with dve.Fori(1, NG) as g:
                group(g, False)
            for t in range(TAIL):
                n = tile_no(NG, t)
                split_next(n, n % RAW)
                previous(NG, t)
                take_tile(n, t % 2, gates[:, 3 * NG + t, :])
            hgrn_out(NG - 1)
            hgrn_lo(NG - 1)
            dve.wait_ge(gate_ready, 4 * NG)

            def merge(b, j):
                ya, yb = hz, hth
                for i, (y, ps) in enumerate(((ya, ps_proj[b]), (yb, ps_lvl[b]))):
                    dve.wait_ge(part_ready, j * 2 + (N_IN + i + 1))
                    nc.vector.tensor_tensor(y, ps[:, 0:T], part[:, i, :], ALU.add).then_inc(y_step, 1)
                for i, y in enumerate((ya, yb)):
                    dve.wait_ge(y_step, j * 4 + i + 1)
                    nc.vector.scalar_tensor_tensor(out=y, in0=at(gates, j + N_BR * i), scalar=1.0, in1=y,
                                                   op0=ALU.add, op1=ALU.mult).then_inc(y_step, 1)
                dve.wait_ge(y_step, j * 4 + 4)
                nc.vector.tensor_tensor(y_sums[b], ya, yb, ALU.add).then_inc(y_sum, 1)

            def split_y(j, b):
                dve.wait_ge(y_hi, j + 1)
                nc.vector.scalar_tensor_tensor(out=at(act_hl, j)[:, T:2 * T], in0=y_sums[b], scalar=0.5,
                                               in1=at(act_hl, j)[:, 0:T].bitcast(F32), op0=ALU.mult,
                                               op1=ALU.subtract).then_inc(y_ready, 1)

            for r in range(RAW):
                split_next(N_IN + r, r)
                if r:
                    split_y(r - 1, (r - 1) % 2)
                merge(r % 2, r)
            with dve.Fori(1, N_BR // RAW) as jj:
                for r in range(RAW):
                    split_next(jj * RAW + (N_IN + r), r)
                    split_y(jj * RAW + (r - 1), (r - 1) % 2)
                    merge(r % 2, jj * RAW + r)
            split_y(N_BR - 1, 1)
            for q in range(N_OUT):
                n = N_IN + N_BR + q
                if q < N_OUT - 1:
                    split_next(n, q % RAW)
                if q % 4 == 3:
                    c = q // 4
                    if c == 0:
                        dve.wait_ge(tail_landed, 3 * 16)
                    for t in range(2):
                        dve.wait_ge(block_sq, 2 * c + t + 1)
                        nc.vector.tensor_tensor(o_tok[:, t, c * 512:(c + 1) * 512], out_bank[c][t][:, :],
                                                post_w[:, c * 512:(c + 1) * 512], ALU.mult).then_inc(out_taken, 1)
            nc.vector.tensor_reduce(ssum, ssq.rearrange("p (t c) -> p t c", t=2), AX.X,
                                    ALU.add).then_inc(fin_step, 1)
            dve.wait_ge(fin_step, 1)
            nc.vector.tensor_scalar(msq, ssum, 1.0 / D, EPS, ALU.mult, ALU.add).then_inc(msq2_ready, 1)
            dve.wait_ge(rstd2_ready, 1)
            dve.wait_ge(out_taken, 8)
            for i in range(8):
                t, c = i // 4, i % 4
                v = o_tok[:, t, c * 512:(c + 1) * 512]
                nc.vector.scalar_tensor_tensor(out=v, in0=v, scalar=rstd[:, t:t + 1],
                                               in1=x_tok[:, t, c * 512:(c + 1) * 512], op0=ALU.mult,
                                               op1=ALU.add).then_inc(out_ready, 1)

        @blk.tensor
        def _(pe):
            def project(n, r, sums, operand, between):
                for h in range(2):
                    if h == 1:
                        between()
                    pe.wait_ge(lo_ready, n * 2 + h + 1)
                    i = (2 * r + h) % HALVES
                    for kk in range(8):
                        k = 8 * h + kk
                        first, last = (k == 0, k == KT - 1) if sums[0] is sums[1] else (kk == 0, kk == 7)
                        if isinstance(n, int) and n == 0:
                            pe.wait_ge(xn_ready, max(k + 1, 2))
                        w = slice(kk * P, (kk + 1) * P)
                        nc.tensor.matmul(sums[h][:, :], w_hi[:, i, w], operand[:, k, :], start=first, stop=False,
                                         skip_group_check=True)
                        ins = nc.tensor.matmul(sums[h][:, 0:T], w_lo[:, i, w], operand[:, k, 0:T], start=False,
                                               stop=last, skip_group_check=True)
                    ins.then_inc(half_used, 1)

            def head_scores(g, a):
                pe.wait_ge(tile_out, tile_no(g, NSLOT_K + 1))
                wait(pe, s_taken, g * 2 + a)
                rows = slice(HEAD * a, HEAD * (a + 1))
                for u in range(2):
                    t = 1 - u
                    ins = nc.tensor.matmul(ps_s[:, u * T:(u + 1) * T], na_q[rows, t * P:(t + 1) * P], na_k[rows, :],
                                           start=True, stop=True)
                ins.then_inc(s_done, 1)

            def turn(v, g, i):
                wait(pe, tr_taken, g * 2 + i)
                for t in range(2):
                    ins = nc.tensor.transpose(ps_tr[:, t * P:(t + 1) * P], v[:, t * P:(t + 1) * P], block[:, 0, :])
                ins.then_inc(tr_done, 1)

            def turn_prob(g, a):
                pe.wait_ge(prob_ready, g * 2 + a + 1)
                wait(pe, pt_taken, g * 2 + a)
                for kt in range(2):
                    for t in range(2):
                        u = 1 - t
                        ins = nc.tensor.transpose(ps_pt[:, kt * T + t * P:kt * T + (t + 1) * P],
                                                  prob[:, a, u * T + kt * P:u * T + (kt + 1) * P], block[:, 0, :])
                ins.then_inc(pt_done, 1)

            def head_out(g, a):
                pe.wait_ge(pt_taken, g * 2 + a + 1)
                pe.wait_ge(tr_taken, g * 2 + 1)
                wait(pe, oa_ready, g)
                for kt in range(2):
                    ins = nc.tensor.matmul(ps_o[HEAD * a:HEAD * (a + 1), 0:T], v_tok[:, kt, HEAD * a:HEAD * (a + 1)],
                                           prob_t[:, a, kt * T:(kt + 1) * T], start=(kt == 0), stop=(kt == 1))
                if a == 1:
                    ins.then_inc(pv_done, 1)

            def level_scores(g, level):
                pe.wait_ge(dec_ready, g * 8 + level + 1)
                wait(pe, lvl_taken, g * 8 + level - 1)
                dst, b = ps_lvl[level % 2], level % 2
                if level == 0:
                    wait(pe, osq_ready, g)
                if level == 1:
                    wait(pe, ob_ready, g)
                for i in range(2):
                    j = 1 - i if level == LEVELS - 1 else i
                    ins = nc.tensor.matmul(dst[:, i * P:(i + 1) * P], k_dec[:, b, i * P:(i + 1) * P],
                                           q_dec[:, b, j * P:(j + 1) * P], start=True, stop=True)
                if level == 0:
                    for i in range(2):
                        c = slice(i * P, (i + 1) * P)
                        ins = nc.tensor.matmul(dst[:, T + i * P:T + (i + 1) * P], key_s[:, c], hq[:, c],
                                               start=True, stop=True)
                ins.then_inc(lvl_done, 1)

            def hgrn_sum(g):
                pe.wait_ge(lvl_taken, g * 8 + 8)
                pe.wait_ge(tr_taken, g * 2 + 2)
                for i in range(2):
                    ins = nc.tensor.matmul(ps_lvl[0][:, 0:T], i_tok[:, i, :], scores_t[:, i * T:(i + 1) * T],
                                           start=(i == 0), stop=(i == 1))
                ins.then_inc(hg_out, 1)

            def square_sum(g):
                pe.wait_ge(osq_ready, g + 1)
                for i in range(2):
                    ins = nc.tensor.matmul(ps_lvl[1][:, i:i + 1], o_sq[:, i * P:(i + 1) * P], ones[:, 0:1],
                                           start=True, stop=True)
                ins.then_inc(ms_done, 1)

            def turn_rst(g):
                pe.wait_ge(rst_spread, g + 1)
                for i in range(2):
                    c = slice(i * P, (i + 1) * P)
                    ins = nc.tensor.transpose(ps_lvl[1][:, c], rst_rows[:, c], block[:, 0, :])
                ins.then_inc(rst_turned, 1)

            def attention(g, s):
                if s == 2:
                    head_scores(g, 0)
                if s == 3:
                    pe.wait_ge(tile_out, tile_no(g, NSLOT_V + 1))
                    turn(na_v, g, 0)
                    head_scores(g, 1)
                if s == 5:
                    turn_prob(g, 0)
                if s == 6:
                    turn_prob(g, 1)
                    head_out(g, 0)
                if s == 7:
                    head_out(g, 1)
                if s == 8:
                    pe.wait_ge(tile_out, tile_no(g, NSLOT_I + 1))
                    turn(i_feat, g, 1)
                if s >= 8:
                    level_scores(g, s - 8)

            def previous(g, s):
                if s < 4:
                    level_scores(g - 1, 4 + s)
                if s == 5:
                    hgrn_sum(g - 1)
                if s == 6:
                    square_sum(g - 1)
                if s == 7:
                    turn_rst(g - 1)

            def group(g, first):
                for s in range(IN_SLOTS):
                    n = tile_no(g, s)
                    wait(pe, tile_out, n - 1)

                    def between():
                        if s == 0:
                            if not first:
                                attention(g - 1, IN_SLOTS - 1)
                        else:
                            if not first:
                                previous(g, s - 1)
                            attention(g, s - 1)

                    project(n, s % RAW, [ps_proj[s % 2]] * 2, act_hl, between)

            pe.wait_ge(const_step, 5)
            pe.wait_ge(vec_landed, 4 * 16)
            nc.tensor.transpose(ps_tr[:, 0:88], vec_rows[:, :], block[0:88, 0, 0:88]).then_inc(vec_turned, 1)
            pe.wait_ge(xs_ready, 2)
            pe.wait_ge(vec_ready, 1)
            for k in range(KT):
                for t in range(2):
                    ins = nc.tensor.transpose(bank[k // 2][:, (k % 2) * T + t * P:(k % 2) * T + (t + 1) * P],
                                              xs_tok[:, t, k * P:(k + 1) * P], block[:, 0, :])
                if k % 2:
                    ins.then_inc(xt_done, 1)

            group(0, True)
            with pe.Fori(1, NG) as g:
                group(g, False)
            for t in range(TAIL):
                n = tile_no(NG, t)
                pe.wait_ge(tile_out, n - 1)
                project(n, n % RAW, [ps_proj[t % 2]] * 2, act_hl,
                        lambda: previous(NG, t - 1) if t else attention(NG - 1, IN_SLOTS - 1))
            previous(NG, TAIL - 1)

            def branch(n, r, j):
                if isinstance(j, int) and j < 2:
                    pe.wait_ge(tile_out, N_IN - 1 + j)
                else:
                    pe.wait_ge(y_sum, j - 1)
                project(n, r, [ps_proj[r % 2], ps_lvl[r % 2]], branch_hl, lambda: pe.wait_ge(ob_lo, NG))

            pe.wait_ge(oa_lo, NG)
            for r in range(RAW):
                branch(N_IN + r, r, r)
            with pe.Fori(1, N_BR // RAW) as jj:
                for r in range(RAW):
                    branch(jj * RAW + (N_IN + r), r, jj * RAW + r)

            for q in range(N_OUT):
                n, r, c = N_IN + N_BR + q, q % RAW, q // 4
                for h in range(2):
                    pe.wait_ge(lo_ready, n * 2 + h + 1)
                    i = (2 * r + h) % HALVES
                    for kk in range(2):
                        k = 4 * r + 2 * h + kk
                        if c == 0:
                            pe.wait_ge(y_ready, k + 1)
                        w = slice(kk * 512, (kk + 1) * 512)
                        for t in range(2):
                            hi, lo = act_hl[:, k, t * P:(t + 1) * P], act_hl[:, k, T + t * P:T + (t + 1) * P]
                            o = out_bank[c][t][:, :]
                            nc.tensor.matmul(o, hi, w_hi[:, i, w], start=(k == 0), stop=False)
                            nc.tensor.matmul(o, hi, w_lo[:, i, w], start=False, stop=False)
                            ins = nc.tensor.matmul(o, lo, w_hi[:, i, w], start=False, stop=(k == KT - 1))
                    ins.then_inc(half_used, 1)


_INS = ["x", "norm_pre_w", "w_in", "b_gate", "na_rel_bias", "hg_lb_logits", "hg_norm_w", "w_branch", "w_out",
        "norm_post_w"]


def kernel(**inputs):
    import numpy as _np
    import concourse.bacc as _bacc
    from concourse.bass_utils import run_bass_kernel_spmd as _run

    nc = _bacc.Bacc("TRN2", target_bir_lowering=False, num_devices=1)
    arrays, args = {}, []
    for name in _INS:
        a = _np.ascontiguousarray(inputs[name])
        arrays[f"in_{name}"] = a
        args.append(nc.dram_tensor(f"in_{name}", a.shape, mybir.dt.from_np(a.dtype), kind="ExternalInput").ap())
    out = nc.dram_tensor("out_0", (1, T, D), F32, kind="ExternalOutput").ap()
    encoder_layer(nc, *args, out)
    r = _run(nc, [arrays], core_ids=[0])
    return r.results[0]["out_0"]
```

```python
from contextlib import ExitStack

import concourse.bass as bass
from concourse import mybir

ALU = mybir.AluOpType
ACT = mybir.ActivationFunctionType
AX = mybir.AxisListType
F32 = mybir.dt.float32
F32R = mybir.dt.float32r
U32 = mybir.dt.uint32

P = 128
T = 256
D = 2048
KT = D // P
NG = 8
GRID_W = 64
ROWS = T // GRID_W
HEAD = 64
WIN_C = 16
BIAS_R, BIAS_C = 15, 31
EPS = 1e-6
NEG = -1e30
IN_SLOTS = 12
TAIL = 8
N_IN = NG * IN_SLOTS + TAIL
N_BR = D // P
LAST_BLOCK = 3
RAW = 4
HALVES = 4
SHARED_BLOCKS = ((0, 2), (0, 3), (1, 2))
LEVELS = 8
WARM_UP = 16
TURN_AHEAD = 8
NSLOT_Q, NSLOT_K, NSLOT_V, NSLOT_Z, NSLOT_F, NSLOT_B, NSLOT_HQ, NSLOT_I, NSLOT_HZ = range(9)
COL_TILE = [0, 8, 16, 24, 40, 48, 32, 56, 64]
GATE_TILE = 72


class Steps:

    def __init__(self, sem, per_group):
        self.sem, self.per_group, self.base, self.k = sem, per_group, 0, 0

    def begin(self, g):
        self.base, self.k = g * self.per_group, 0

    def resume(self, g):
        self.base = g * self.per_group

    def done(self, instruction):
        instruction.then_inc(self.sem, 1)
        self.k += 1

    def settle(self, engine, but=0):
        engine.wait_ge(self.sem, self.base + (self.k - but))

    def end(self):
        assert self.k == self.per_group, (self.k, self.per_group)


def encoder_layer(nc, x, norm_pre_w, w_in, b_gate, na_rel_bias, hg_lb_logits, hg_norm_w, w_branch,
                  w_out, norm_post_w, out):
    w_in_v = w_in[0].rearrange("(k p) n -> p k n", p=P)
    w_branch_v = w_branch[0].rearrange("(k p) n -> p k n", p=P)
    w_out_v = w_out[0].rearrange("(k p) n -> p k n", p=P)

    with ExitStack() as ctx:
        def sb(name, shape, dt=F32):
            return ctx.enter_context(nc.sbuf_tensor(name, shape, dt))

        def sem(name):
            return ctx.enter_context(nc.semaphore(name))

        act_hl = sb("act_hl", [P, KT, 2 * T], F32R)
        branch_hl = sb("branch_hl", [P, 2 * NG, 2 * T], F32R)
        qk_hi, qk_lo = branch_hl[:, NG - 1, :], branch_hl[:, 2 * NG - 1, :]
        raw = sb("raw", [P, RAW, 2 * 1024])
        w_hi = sb("w_hi", [P, HALVES, 1024], F32R)
        w_lo = sb("w_lo", [P, HALVES, 1024], F32R)
        big = sb("big", [P, 32, T])
        gates = big
        x_tok = big[:, 0:16, :].rearrange("p (t a) c -> p t (a c)", t=2)
        xs_tok = big[:, 16:32, :].rearrange("p (t a) c -> p t (a c)", t=2)
        o_tok = xs_tok
        bias_t = sb("bias_t", [P, 2, 6 * GRID_W])
        part = sb("part", [P, 2, T])
        na = sb("na", [P, 5, T])
        na_q, na_k, na_v, na_z, na_th = (na[:, i, :] for i in range(5))
        v_tok = sb("v_tok", [P, 2, P])
        wide = sb("wide", [P, 4, 2 * T])
        prob, prob_t = wide[:, 0:2, :], wide[:, 2:4, :]
        hg = sb("hg", [P, 14, T])
        pre_f, suf_f, suf_b, pre_b, hq, key_f, key_b, key_s, i_feat, hz, hth, o_h, o_sq, rst_rows = (
            hg[:, i, :] for i in range(14))
        q_dec = sb("q_dec", [P, 2, T])
        k_dec = sb("k_dec", [P, 2, T])
        scores_t = sb("scores_t", [P, 4 * P])
        i_tok = sb("i_tok", [P, 2, P])
        block = sb("block", [P, 7, P])
        ones = sb("ones", [P, P])
        win = sb("win", [P, 2, GRID_W])
        vec_rows = sb("vec_rows", [88, P])
        vec = sb("vec", [P, 88])
        small = sb("small", [P, 128])
        lb0, lb1, lb_m, lb_r = (small[:, 16 * i:16 * i + 16] for i in range(4))
        half_open = small[:, 64:80]
        half_shut = small[:, 80:96]
        mid = small[:, 96:112]
        half_hgw = small[:, 112:120]
        small2 = sb("small2", [P, 64])
        half_bg = small2[:, 0:32]
        ssq = small2[:, 32:40]
        ssum, msq, rstd = small2[:, 40:42], small2[:, 42:44], small2[:, 44:46]
        nmax, rsum, rinv = small2[:, 46:50], small2[:, 50:54], small2[:, 54:58]
        neg_half = small2[:, 58:59]
        hg_ms, hg_rst = small2[:, 59:61], small2[:, 61:63]
        y_sums = (o_sq, o_h)
        post_w = wide[:, :, :].rearrange("p a b -> p (a b)")

        psum = ctx.enter_context(nc.psum_tensor("psum", [P, 8, 512], F32))
        bank = [psum[:, i, :] for i in range(8)]
        ps_s, ps_pt, ps_o, ps_tr = bank[0:4]
        ps_proj, ps_lvl = bank[4:6], bank[6:8]
        turn_bank = bank[5:8] + bank[0:4] + bank[5:6]

        raw_landed = [sem(f"raw_landed{i}") for i in range(RAW)]
        hi_ready = sem("hi_ready")
        lo_ready = sem("lo_ready")
        half_used = sem("half_used")
        part_ready = sem("part_ready")
        tile_out = sem("tile_out")
        vec_landed, x0_landed, x1_landed = sem("vec_landed"), sem("x0_landed"), sem("x1_landed")
        const_step, ones_ready, win_ready = sem("const_step"), sem("ones_ready"), sem("win_ready")
        masks_ready = sem("masks_ready")
        vec_turned, vec_ready = sem("vec_turned"), sem("vec_ready")
        setup_step = sem("setup_step")
        ss0_ready, msq_ready, rstd_ready = sem("ss0_ready"), sem("msq_ready"), sem("rstd_ready")
        xs_ready, xt_done, xhi_ready, xn_ready = (
            sem("xs_ready"), sem("xt_done"), sem("xhi_ready"), sem("xn_ready"))
        lbm_ready, lbe_ready = sem("lbm_ready"), sem("lbe_ready")
        bias_landed, bias_ready = sem("bias_landed"), sem("bias_ready")
        qk_hi_ready, qk_lo_ready = sem("qk_hi_ready"), sem("qk_lo_ready")
        s_done, s_taken = sem("s_done"), sem("s_taken")
        max_ready, exp_ready, prob_ready = sem("max_ready"), sem("exp_ready"), sem("prob_ready")
        tr_done, tr_taken = sem("tr_done"), sem("tr_taken")
        pt_done, pt_taken = sem("pt_done"), sem("pt_taken")
        pv_done, nz_tanh = sem("pv_done"), sem("nz_tanh")
        oa_ready, oa_hi, oa_lo = sem("oa_ready"), sem("oa_hi"), sem("oa_lo")
        na_step = sem("na_step")
        f_tanh, b_tanh, hz_tanh = sem("f_tanh"), sem("b_tanh"), sem("hz_tanh")
        dec_ready, lvl_done, lvl_taken = sem("dec_ready"), sem("lvl_done"), sem("lvl_taken")
        hg_out, osq_ready, ms_done = sem("hg_out"), sem("osq_ready"), sem("ms_done")
        ms_ready, rst_ready, rst_spread, rst_turned = (
            sem("ms_ready"), sem("rst_ready"), sem("rst_spread"), sem("rst_turned"))
        ob_ready, ob_hi, ob_lo = sem("ob_ready"), sem("ob_hi"), sem("ob_lo")
        hg_step, ob_step = sem("hg_step"), sem("ob_step")
        gate_ready = sem("gate_ready")
        y_sum, y_hi, y_ready, y_step = sem("y_sum"), sem("y_hi"), sem("y_ready"), sem("y_step")
        tail_landed, block_sq, out_taken = sem("tail_landed"), sem("block_sq"), sem("out_taken")
        fin_step, msq2_ready, rstd2_ready = sem("fin_step"), sem("msq2_ready"), sem("rstd2_ready")
        out_ready, pool_out_ready, out_stored = sem("out_ready"), sem("pool_out_ready"), sem("out_stored")
        scaled = sem("scaled")

        def wait(engine, semaphore, value):
            if isinstance(value, int) and value <= 0:
                return
            engine.wait_ge(semaphore, value)

        def loop(engine, start, end):
            return nc.Fori(start, end, engines=[engine.engine], hint_back_edge=True)

        def store(engine, t, c):
            engine.dma_start(out[0, t * P:(t + 1) * P, c * 512:(c + 1) * 512],
                             o_tok[:, t, c * 512:(c + 1) * 512]).then_inc(out_stored, 16)

        def tile_no(g, s):
            return g * IN_SLOTS + s

        def raw_count(n4, r):
            return n4 * 16 + 16

        def at(ap, i):
            if isinstance(i, int):
                return ap[:, i]
            return ap[:, bass.ds(i, 1)].rearrange("p a b -> p (a b)")

        def block_columns(ap, c):
            return ap[:, 512 * c:512 * (c + 1)] if isinstance(c, int) else ap[:, bass.ds(c * 512, 512)]

        def column(ap, i):
            return ap[:, i:i + 1] if isinstance(i, int) else ap[:, bass.ds(i, 1)]

        def pairs(ap, half):
            return ap.rearrange("p (n two h) -> p n two h", two=2, h=half)

        def both_tiles(ap):
            return bass.AP(ap.tensor, ap.offset, [list(ap.ap[0]), [3 * P, 2], [1, P]])

        blk = ctx.enter_context(nc.Block())

        @blk.sync
        def _(sp):
            def load(r, src, n):
                wait(sp, lo_ready, n * 2 - 2 * RAW + 2)
                dst = raw[:, r, :]
                k = src.shape[1]
                sp.dma_start(dst.rearrange("p (k c) -> p k c", k=k), src).then_inc(raw_landed[r], 16)

            def load_bias(g):
                wait(sp, s_taken, g * 2)
                for parity in range(2):
                    for a in range(2):
                        src = bass.AP(na_rel_bias.tensor,
                                      (g * 2 + a) * (BIAS_R * BIAS_C) + (5 - parity) * BIAS_C + 15 - (GRID_W - 1),
                                      [[1, GRID_W], [BIAS_C, 6], [1, GRID_W]])
                        dst = bias_t[GRID_W * parity:GRID_W * (parity + 1), a, :]
                        sp.dma_start(dst.rearrange("p (m c) -> p m c", m=6), src).then_inc(bias_landed, 16)

            def group(g):
                for s in range(IN_SLOTS):
                    if s == 1:
                        load_bias(g)
                    col = g + COL_TILE[s] if s < 9 else g * 3 + (GATE_TILE + s - 9)
                    cols = slice(col * P, col * P + P) if isinstance(g, int) else bass.ds(col * P, P)
                    load(s % RAW, w_in_v[:, :, cols], tile_no(g, s))

            sp.dma_start(x_tok[:, 0, :], x[0, 0:P, :]).then_inc(x0_landed, 16)
            sp.dma_start(x_tok[:, 1, :], x[0, P:T, :]).then_inc(x1_landed, 16)
            group(0)
            with loop(sp, 1, NG) as g:
                group(g)
            for t in range(TAIL):
                col = GATE_TILE + 3 * NG + t
                load(t % RAW, w_in_v[:, :, col * P:col * P + P], tile_no(NG, t))
            with loop(sp, 0, N_BR // RAW) as jj:
                for r in range(RAW):
                    load(r, w_branch_v[:, :, bass.ds(jj * (RAW * P) + r * P, P)], jj * RAW + (N_IN + r))
            with loop(sp, 0, 4) as c:
                for r in range(4):
                    load(r, w_out_v[:, 4 * r:4 * r + 4, bass.ds(c * 512, 512)], c * RAW + (N_IN + N_BR + r))
            for i, (t, c) in enumerate(((0, 0), (0, 1), (1, 0), (1, 1), (1, 3))):
                sp.wait_ge(out_ready, i + 1)
                store(sp, t, c)
            sp.wait_ge(out_stored, 8 * 16)

        @blk.gpsimd
        def _(pool):
            nc.gpsimd.memset(ones[:, :], 1.0).then_inc(const_step, 1)
            nc.gpsimd.memset(win[:, :, :], 0.0).then_inc(const_step, 1)
            nc.gpsimd.memset(neg_half, -0.5).then_inc(const_step, 1)
            pool.wait_ge(const_step, 1)
            steps = 3
            for i in range(7):
                if i == 1:
                    for t in range(2):
                        pool.wait_ge(msq_ready, t + 1)
                        nc.gpsimd.tensor_tensor(rstd[:, t:t + 1], msq[:, t:t + 1], neg_half,
                                                ALU.pow).then_inc(rstd_ready, 1)
                    for h in range(2):
                        pool.wait_ge(hi_ready, h + 1)
                        nc.gpsimd.tensor_tensor(w_lo[:, h, :], raw[:, 0, 1024 * h:1024 * (h + 1)],
                                                w_hi[:, h, :].bitcast(F32), ALU.subtract).then_inc(lo_ready, 1)
                n = 1 << i
                v = block[:, i, :].rearrange("p (b w) -> p b w", w=n)
                src = ones[:, :].rearrange("p (b w) -> p b w", w=n)
                nc.gpsimd.affine_select(out=v, in_=src, compare_op=ALU.is_ge, fill=0.0, base=0,
                                        pattern=[[-n, P // n], [0, n]], channel_multiplier=1).then_inc(const_step, 1)
                steps += 1
                pool.wait_ge(const_step, steps)
                nc.gpsimd.affine_select(out=v, in_=v, compare_op=ALU.is_ge, fill=0.0, base=n - 1,
                                        pattern=[[n, P // n], [0, n]], channel_multiplier=-1).then_inc(const_step, 1)
                steps += 1
            pool.wait_ge(const_step, steps)
            for sel in ((win[:, :, 0:GRID_W - WIN_C], 1, -(GRID_W - 1 - WIN_C // 2)),
                        (win[:, :, WIN_C:GRID_W], -1, GRID_W - 1 + WIN_C // 2 - 1 - WIN_C)):
                v, sign, base = sel
                nc.gpsimd.affine_select(out=v, in_=v, compare_op=ALU.is_ge, fill=NEG, base=base,
                                        pattern=[[-GRID_W * sign, 2], [sign, GRID_W - WIN_C]],
                                        channel_multiplier=sign).then_inc(const_step, 1)
                steps += 1
                pool.wait_ge(const_step, steps)
            for base, step, mult in ((0, -GRID_W, 1), (GRID_W - 1, GRID_W, -1)):
                nc.gpsimd.affine_select(out=win[:, :, :], in_=win[:, :, :], compare_op=ALU.is_ge, fill=0.0,
                                        base=base, pattern=[[step, 2], [0, GRID_W]],
                                        channel_multiplier=mult).then_inc(const_step, 1)
                steps += 1
                pool.wait_ge(const_step, steps)
            nc.gpsimd.tensor_tensor(win[:, 0, :], win[:, 0, :], win[:, 1, :], ALU.add).then_inc(win_ready, 1)
            pool.wait_ge(win_ready, 1)

            def mask_bias(g):
                pool.wait_ge(bias_landed, g * 64 + 64)
                v = bias_t[:, :, :].rearrange("p a (m c) -> p (a m) c", c=GRID_W)
                w = win[:, 0:1, :].to_broadcast([P, 12, GRID_W])
                nc.gpsimd.tensor_tensor(v, v, w, ALU.add).then_inc(bias_ready, 1)

            def power(g):
                pool.wait_ge(ms_ready, g + 1)
                nc.gpsimd.tensor_tensor(hg_rst, hg_ms, neg_half.to_broadcast([P, 2]), ALU.pow).then_inc(rst_ready, 1)

            mask_bias(0)
            with loop(pool, 1, NG) as g:
                mask_bias(g)
                power(g - 1)
            power(NG - 1)
            def out_power(t):
                pool.wait_ge(msq2_ready, t + 1)
                nc.gpsimd.tensor_tensor(rstd[:, t:t + 1], msq[:, t:t + 1], neg_half, ALU.pow).then_inc(rstd2_ready, 1)

            def add_scaled(i):
                t, c = SHARED_BLOCKS[i]
                pool.wait_ge(scaled, i + 1)
                v = block_columns(o_tok[:, t, :], c)
                nc.gpsimd.tensor_tensor(v, v, block_columns(x_tok[:, t, :], c), ALU.add).then_inc(pool_out_ready, 1)

            out_power(0)
            add_scaled(0)
            out_power(1)
            add_scaled(1)
            add_scaled(2)

        @blk.scalar
        def _(act):
            def split_hi(n, r, n4, h):
                if h == 0:
                    act.wait_ge(raw_landed[r], raw_count(n4, r))
                wait(act, half_used, n * 2 + h - HALVES + 1)
                nc.scalar.activation(w_hi[:, (2 * r + h) % HALVES, :], raw[:, r, 1024 * h:1024 * (h + 1)],
                                     ACT.Copy).then_inc(hi_ready, 1)

            def split_next(n, n4, r):
                r1, c1 = (r + 1) % RAW, n4 + (r + 1) // RAW
                split_hi(n + 1, r1, c1, 0)
                split_hi(n + 1, r1, c1, 1)

            def take_part(n, b):
                act.wait_ge(half_used, n * 2 + 2)
                nc.scalar.activation(part[:, b, :], ps_proj[b][:, T:2 * T], ACT.Copy).then_inc(part_ready, 1)

            def gate_tanh(i, n):
                act.wait_ge(tile_out, n + 1)
                v = at(gates, i)
                nc.scalar.activation(v, v, ACT.Tanh, scale=0.5, bias=column(half_bg, i)).then_inc(gate_ready, 1)

            def tanh_half(v, n, semaphore):
                act.wait_ge(tile_out, n + 1)
                nc.scalar.activation(v[0], v[1], ACT.Tanh, scale=0.5).then_inc(semaphore, 1)

            def exp_head(g, a):
                act.wait_ge(max_ready, g * 2 + a + 1)
                for u in range(2):
                    v = prob[:, a, u * T:(u + 1) * T]
                    i = 2 * a + u
                    nc.scalar.activation(v, v, ACT.Exp, bias=nmax[:, i:i + 1],
                                         accum_out=rsum[:, i:i + 1]).then_inc(exp_ready, 1)

            def take_prob_t(g, a):
                act.wait_ge(pt_done, g * 2 + a + 1)
                nc.scalar.activation(prob_t[:, a, :], ps_pt[:, :], ACT.Copy).then_inc(pt_taken, 1)

            def attention(g, s):
                n = tile_no(g, s)
                if s == 2:
                    act.wait_ge(tile_out, tile_no(g, NSLOT_K + 1))
                    nc.scalar.activation(qk_hi, na[:, 0:2, :].rearrange("p a b -> p (a b)"),
                                         ACT.Copy).then_inc(qk_hi_ready, 1)
                if s == 3:
                    exp_head(g, 0)
                if s == 4:
                    act.wait_ge(tr_done, g * 2 + 1)
                    nc.scalar.activation(v_tok[:, :, :].rearrange("p a b -> p (a b)"), ps_tr[:, 0:T],
                                         ACT.Copy).then_inc(tr_taken, 1)
                    tanh_half((na_th, na_z), n - 1, nz_tanh)
                    exp_head(g, 1)
                if s == 5:
                    tanh_half((pre_f, pre_f), n - 1, f_tanh)
                if s == 6:
                    take_prob_t(g, 0)
                    tanh_half((suf_b, suf_b), n - 1, b_tanh)
                if s == 7:
                    take_prob_t(g, 1)
                if s == 9:
                    act.wait_ge(tr_done, g * 2 + 2)
                    nc.scalar.activation(i_tok[:, :, :].rearrange("p a b -> p (a b)"), ps_tr[:, 0:T],
                                         ACT.Copy).then_inc(tr_taken, 1)
                    tanh_half((hth, hz), n - 1, hz_tanh)
                    act.wait_ge(oa_ready, g + 1)
                    nc.scalar.activation(at(branch_hl, g)[:, 0:T], na_th, ACT.Copy).then_inc(oa_hi, 1)
                if s == 10:
                    gate_tanh(g * 3, n - 1)
                if s == 11:
                    gate_tanh(g * 3 + 1, n - 1)

            def out_square(g):
                act.wait_ge(hg_out, g + 1)
                nc.scalar.activation(o_h, ps_lvl[0][:, 0:T], ACT.Copy)
                nc.scalar.activation(o_sq, ps_lvl[0][:, 0:T], ACT.Square).then_inc(osq_ready, 1)

            def hgrn_hi(g):
                act.wait_ge(ob_ready, g + 1)
                nc.scalar.activation(at(branch_hl, g + NG)[:, 0:T], o_h, ACT.Copy).then_inc(ob_hi, 1)

            def previous(g, s):
                if s == 0:
                    gate_tanh((g - 1) * 3 + 2, tile_no(g, -1))
                if s == 6:
                    out_square(g - 1)
                if s == 9:
                    hgrn_hi(g - 1)

            def group(g, first):
                for s in range(IN_SLOTS):
                    n, n4, r = tile_no(g, s), g * 3 + s // RAW, s % RAW
                    split_next(n, n4, r)
                    if not first:
                        previous(g, s)
                    elif s == 1:
                        act.wait_ge(lbm_ready, 1)
                        nc.scalar.activation(lb0, lb0, ACT.Exp)
                        nc.scalar.activation(lb1, lb1, ACT.Exp).then_inc(lbe_ready, 1)
                    attention(g, s)
                    take_part(n, s % 2)

            rows = ((0, hg_lb_logits.rearrange("l d (h c) -> (l d h) c", c=P)),
                    (32, b_gate.rearrange("o (h c) -> (o h) c", c=P)),
                    (64, norm_pre_w.rearrange("o (h c) -> (o h) c", c=P)),
                    (80, hg_norm_w.rearrange("o (h c) -> (o h) c", c=P)))
            for r0, src in rows:
                act.dma_start(vec_rows[r0:r0 + src.shape[0], :], src).then_inc(vec_landed, 16)
            act.wait_ge(x0_landed, 16)
            nc.scalar.activation(xs_tok[:, 0, :], x_tok[:, 0, :], ACT.Square,
                                 accum_out=ssq[:, 0:1]).then_inc(ss0_ready, 1)
            act.wait_ge(x1_landed, 16)
            nc.scalar.activation(xs_tok[:, 1, 0:D // 2], x_tok[:, 1, 0:D // 2], ACT.Square,
                                 accum_out=ssq[:, 2:3]).then_inc(ss0_ready, 1)
            split_hi(0, 0, 0, 0)
            act.wait_ge(vec_turned, 1)
            nc.scalar.activation(vec[:, :], ps_tr[:, 0:88], ACT.Copy).then_inc(vec_ready, 1)
            split_hi(0, 0, 0, 1)
            act.wait_ge(vec_ready, 1)
            for k in range(KT):
                act.wait_ge(xt_done, k // 2 + 1)
                nc.scalar.activation(act_hl[:, k, 0:T], turn_bank[k // 2][:, (k % 2) * T:(k % 2 + 1) * T], ACT.Copy,
                                     scale=vec[:, 64 + k:65 + k]).then_inc(xhi_ready, 1)

            group(0, True)
            with loop(act, 1, NG) as g:
                group(g, False)
            for t in range(TAIL):
                n = tile_no(NG, t)
                split_next(n, n // RAW, n % RAW)
                if t > 0:
                    gate_tanh(3 * NG + t - 1, n - 1)
                previous(NG, t)
                take_part(n, t % 2)
            gate_tanh(3 * NG + TAIL - 1, tile_no(NG, TAIL - 1))
            hgrn_hi(NG - 1)

            def take_branch(n, b, j):
                act.wait_ge(half_used, n * 2 + 1)
                wait(act, y_sum, j)
                nc.scalar.activation(part[:, 0, :], ps_proj[b][:, T:2 * T], ACT.Copy).then_inc(part_ready, 1)
                act.wait_ge(half_used, n * 2 + 2)
                nc.scalar.activation(part[:, 1, :], ps_lvl[b][:, T:2 * T], ACT.Copy).then_inc(part_ready, 1)

            def split_y(j, b):
                act.wait_ge(y_sum, j + 1)
                nc.scalar.activation(at(act_hl, j)[:, 0:T], y_sums[b], ACT.Copy,
                                     scale=0.5).then_inc(y_hi, 1)

            act.wait_ge(tile_out, N_IN)
            act.wait_ge(pv_done, NG)
            act.dma_start(post_w, norm_post_w.partition_broadcast(P)).then_inc(tail_landed, 16)
            for r in range(RAW):
                split_next(N_IN + r, N_IN // RAW, r)
                if r:
                    split_y(r - 1, (r - 1) % 2)
                take_branch(N_IN + r, r % 2, r)
            with loop(act, 1, N_BR // RAW) as jj:
                for r in range(RAW):
                    n = jj * RAW + (N_IN + r)
                    split_next(n, jj + N_IN // RAW, r)
                    split_y(jj * RAW + (r - 1), (r - 1) % 2)
                    take_branch(n, r % 2, jj * RAW + r)
            split_y(N_BR - 1, 1)
            for t in range(2):
                act.dma_start(x_tok[:, t, :], x[0, t * P:(t + 1) * P, :]).then_inc(tail_landed, 16)

            def block_square(c, t, early=0):
                act.wait_ge(half_used, c * (2 * RAW) + (2 * (N_IN + N_BR + RAW) - early))
                nc.scalar.activation(hg[:, 2 * t:2 * t + 2, :].rearrange("p a b -> p (a b)"), at(psum, c * 2 + t),
                                     ACT.Square, accum_out=column(ssq, c + 4 * t)).then_inc(block_sq, 1)

            with loop(act, 0, LAST_BLOCK) as c:
                for r in range(RAW):
                    split_next(c * RAW + (N_IN + N_BR + r), c + (N_IN + N_BR) // RAW, r)
                for t in range(2):
                    block_square(c, t)
                act.wait_ge(block_sq, c * 2 + 2)
            for r in range(RAW - 1):
                split_next(LAST_BLOCK * RAW + N_IN + N_BR + r, LAST_BLOCK + (N_IN + N_BR) // RAW, r)

            def scale(i):
                t, c = SHARED_BLOCKS[i]
                act.wait_ge(rstd2_ready, t + 1)
                v = block_columns(o_tok[:, t, :], c)
                nc.scalar.activation(v, v, ACT.Copy, scale=rstd[:, t:t + 1]).then_inc(scaled, 1)

            block_square(LAST_BLOCK, 0, early=1)
            act.wait_ge(out_taken, 6)
            scale(0)
            block_square(LAST_BLOCK, 1)
            act.wait_ge(out_taken, 7)
            scale(1)
            scale(2)
            for i, (t, c) in enumerate(SHARED_BLOCKS):
                act.wait_ge(pool_out_ready, i + 1)
                store(act, t, c)

        @blk.vector
        def _(dve):
            na_s, hg_s, ob_s = Steps(na_step, 3), Steps(hg_step, 2 * 2 + 1 + 1 + 4 * (LEVELS - 1)), Steps(ob_step, 2)

            def split_lo(n, r, h):
                dve.wait_ge(hi_ready, n * 2 + h + 1)
                i = (2 * r + h) % HALVES
                nc.vector.tensor_tensor(w_lo[:, i, :], raw[:, r, 1024 * h:1024 * (h + 1)],
                                        w_hi[:, i, :].bitcast(F32), ALU.subtract).then_inc(lo_ready, 1)

            def split_next(n, r):
                split_lo(n + 1, (r + 1) % RAW, 0)
                split_lo(n + 1, (r + 1) % RAW, 1)

            def take_tile(n, b, dst):
                dve.wait_ge(part_ready, n + 1)
                if dst is na_q:
                    dst = na_q.rearrange("p (r c) -> p r c", c=GRID_W)[:, :, ::-1]
                    src = ps_proj[b][:, 0:T].rearrange("p (r c) -> p r c", c=GRID_W)
                    prt = part[:, b, :].rearrange("p (r c) -> p r c", c=GRID_W)
                else:
                    src, prt = ps_proj[b][:, 0:T], part[:, b, :]
                nc.vector.tensor_tensor(dst, src, prt, ALU.add).then_inc(tile_out, 1)

            def scores_and_max(g, a):
                dve.wait_ge(s_done, g * 2 + a + 1)
                if a == 0:
                    dve.wait_ge(bias_ready, g + 1)
                bias = bass.AP(bias_t[:, :, :].tensor, a * 6 * GRID_W, [[12 * GRID_W, P], [2 * GRID_W, 2], [1, T]])
                pv = prob[:, a, :].rearrange("p (u k) -> p u k", u=2)
                nc.vector.scalar_tensor_tensor(out=pv, in0=ps_s[:, :].rearrange("p (u k) -> p u k", u=2),
                                               scalar=HEAD ** -0.5, in1=bias, op0=ALU.mult,
                                               op1=ALU.add).then_inc(s_taken, 1)
                dve.wait_ge(s_taken, g * 2 + a + 1)
                nc.vector.tensor_reduce(nmax[:, 2 * a:2 * a + 2], pv, AX.X, ALU.max,
                                        negate=True).then_inc(max_ready, 1)

            def normalise(g, a):
                dve.wait_ge(exp_ready, g * 4 + 2 * a + 2)
                na_s.done(nc.vector.reciprocal(rinv[:, 2 * a:2 * a + 2], rsum[:, 2 * a:2 * a + 2]))
                na_s.settle(dve)
                for u in range(2):
                    v = prob[:, a, u * T:(u + 1) * T]
                    ins = nc.vector.tensor_scalar(v, v, rinv[:, 2 * a + u:2 * a + u + 1], None, ALU.mult)
                ins.then_inc(prob_ready, 1)

            def gate_constants(v, key, semaphore, g, direction):
                dve.wait_ge(semaphore, g + 1)
                i = g + 8 * direction
                hg_s.done(nc.vector.tensor_scalar(key, v, column(half_shut, i), column(half_open, i),
                                                  ALU.mult, ALU.add))
                hg_s.done(nc.vector.tensor_scalar(v, v, column(half_open, i), column(mid, i), ALU.mult, ALU.add))

            def grow(half):
                def bc(ap, side, pos):
                    return pairs(ap, half)[:, :, side, pos:pos + 1].to_broadcast([P, T // (2 * half), half])
                for i, (dst, side, src) in enumerate((
                        (suf_f, 0, bc(pre_f, 1, half - 1)), (pre_b, 1, bc(suf_b, 0, 0)),
                        (pre_f, 1, bc(pre_f, 0, half - 1)), (suf_b, 0, bc(suf_b, 1, 0)))):
                    if i >= 2:
                        hg_s.settle(dve, but=1)
                    d = pairs(dst, half)[:, :, side, :]
                    hg_s.done(nc.vector.tensor_tensor(d, d, src, ALU.mult))

            def decayed(g, level):
                half, b = 1 << level, level % 2
                hg_s.settle(dve)
                if level > 0:
                    dve.wait_ge(dec_ready, g * 8 + level)
                    grow(half // 2)
                    hg_s.settle(dve)
                for dst, side, v, w in ((q_dec, 1, hq, pre_f), (q_dec, 0, hq, suf_b),
                                        (k_dec, 0, key_f, suf_f), (k_dec, 1, key_b, pre_b)):
                    ins = nc.vector.tensor_tensor(*(pairs(i, half)[:, :, side, :] for i in (dst[:, b, :], v, w)),
                                                  ALU.mult)
                ins.then_inc(dec_ready, 1)

            def take_and_decay(g, level):
                dve.wait_ge(lvl_done, g * 8 + level + 1)
                src = ps_lvl[level % 2]
                if level == LEVELS - 1:
                    nc.vector.tensor_copy(scores_t[:, P:3 * P], src[:, 0:T]).then_inc(lvl_taken, 1)
                    hg_s.end()
                    return
                data = src[:, 0:T].rearrange("p (a t) -> p a t", a=2)
                if level == 0:
                    hg_s.done(nc.vector.tensor_copy(both_tiles(scores_t[:, :]), data))
                    data = src[:, T:2 * T].rearrange("p (a t) -> p a t", a=2)
                else:
                    dve.wait_ge(lvl_taken, g * 8 + level)
                decayed(g, level + 1)
                mask = block[:, level:level + 1, :].bitcast(U32).to_broadcast([P, 2, P])
                nc.vector.copy_predicated(both_tiles(scores_t[:, :]), mask, data).then_inc(lvl_taken, 1)

            def attention(g, s):
                if s == 2:
                    dve.wait_ge(qk_hi_ready, g + 1)
                    nc.vector.tensor_tensor(qk_lo, na[:, 0:2, :].rearrange("p a b -> p (a b)"), qk_hi.bitcast(F32),
                                            ALU.subtract).then_inc(qk_lo_ready, 1)
                if s == 3:
                    na_s.begin(g)
                    scores_and_max(g, 0)
                if s == 4:
                    scores_and_max(g, 1)
                    normalise(g, 0)
                if s == 5:
                    normalise(g, 1)
                if s == 6:
                    hg_s.begin(g)
                    gate_constants(pre_f, key_f, f_tanh, g, 0)
                if s == 7:
                    gate_constants(suf_b, key_b, b_tanh, g, 1)
                    nc.vector.memset(suf_f, 1.0)
                    nc.vector.memset(pre_b, 1.0)
                    hg_s.settle(dve)
                    hg_s.done(nc.vector.tensor_tensor(key_s, key_f, key_b, ALU.add))
                if s == 8:
                    dve.wait_ge(nz_tanh, g + 1)
                    na_s.done(nc.vector.scalar_tensor_tensor(out=na_th, in0=na_th, scalar=1.0, in1=na_z,
                                                             op0=ALU.add, op1=ALU.mult))
                    dve.wait_ge(pv_done, g + 1)
                    na_s.settle(dve)
                    v = na_th.rearrange("p (r c) -> p r c", c=GRID_W)
                    o = ps_o[:, 0:T].rearrange("p (r c) -> p r c", c=GRID_W)[:, :, ::-1]
                    nc.vector.scalar_tensor_tensor(out=v, in0=v, scalar=0.5, in1=o, op0=ALU.mult,
                                                   op1=ALU.mult).then_inc(oa_ready, 1)
                    dve.wait_ge(tile_out, tile_no(g, NSLOT_HQ + 1))
                    decayed(g, 0)
                if s >= 9:
                    take_and_decay(g, s - 9)
                if s == 10:
                    dve.wait_ge(oa_hi, g + 1)
                    nc.vector.tensor_tensor(at(branch_hl, g)[:, T:2 * T], na_th,
                                            at(branch_hl, g)[:, 0:T].bitcast(F32), ALU.subtract).then_inc(oa_lo, 1)

            def mean_square(g):
                dve.wait_ge(ms_done, g + 1)
                nc.vector.tensor_scalar(hg_ms, ps_lvl[1][:, 0:2], 1.0 / P, EPS, ALU.mult, ALU.add).then_inc(ms_ready, 1)
                dve.wait_ge(rst_ready, g + 1)
                for i in range(2):
                    ins = nc.vector.tensor_scalar(rst_rows[:, i * P:(i + 1) * P], ones[:, :], hg_rst[:, i:i + 1], None,
                                                  ALU.mult)
                ins.then_inc(rst_spread, 1)

            def hgrn_out(g):
                ob_s.begin(g)
                dve.wait_ge(hz_tanh, g + 1)
                ob_s.done(nc.vector.scalar_tensor_tensor(out=hth, in0=hth, scalar=1.0, in1=hz, op0=ALU.add,
                                                         op1=ALU.mult))
                dve.wait_ge(rst_turned, g + 1)
                ob_s.done(nc.vector.scalar_tensor_tensor(out=o_h, in0=o_h, scalar=column(half_hgw, g),
                                                         in1=ps_lvl[1][:, 0:T],
                                                         op0=ALU.mult, op1=ALU.mult))
                ob_s.settle(dve)
                ob_s.end()
                nc.vector.tensor_tensor(o_h, o_h, hth, ALU.mult).then_inc(ob_ready, 1)

            def hgrn_lo(g):
                dve.wait_ge(ob_hi, g + 1)
                nc.vector.tensor_tensor(at(branch_hl, g + NG)[:, T:2 * T], o_h,
                                        at(branch_hl, g + NG)[:, 0:T].bitcast(F32), ALU.subtract).then_inc(ob_lo, 1)

            def previous(g, s):
                if s == 0:
                    hg_s.resume(g - 1)
                if s < 5:
                    take_and_decay(g - 1, 3 + s)
                if s == 7:
                    mean_square(g - 1)
                if s == 8:
                    hgrn_out(g - 1)
                if s == 10:
                    hgrn_lo(g - 1)

            k = 0

            def link(ins):
                nonlocal k
                ins.then_inc(setup_step, 1)
                k += 1
                dve.wait_ge(setup_step, k)

            def gate_set_up():
                dve.wait_ge(vec_ready, 1)
                link(nc.vector.tensor_tensor(lb_m, vec[:, 0:16], vec[:, 16:32], ALU.max))
                nc.vector.tensor_tensor(lb0, vec[:, 0:16], lb_m, ALU.subtract)
                nc.vector.tensor_tensor(lb1, vec[:, 16:32], lb_m, ALU.subtract).then_inc(lbm_ready, 1)
                nc.vector.tensor_scalar(half_bg, vec[:, 32:64], 0.5, None, ALU.mult)
                nc.vector.tensor_scalar(half_hgw, vec[:, 80:88], 0.5, None, ALU.mult).then_inc(vec_ready, 1)
                dve.wait_ge(lbe_ready, 1)
                link(nc.vector.tensor_tensor(lb_r, lb0, lb1, ALU.add))
                link(nc.vector.reciprocal(lb_r, lb_r))
                link(nc.vector.tensor_tensor(lb0, lb0, lb_r, ALU.mult))
                link(nc.vector.tensor_tensor(lb1, lb1, lb_r, ALU.mult))
                link(nc.vector.tensor_scalar(half_open, lb1, 0.5, None, ALU.mult))
                nc.vector.tensor_scalar(half_shut, lb1, -0.5, None, ALU.mult)
                link(nc.vector.tensor_tensor(mid, lb0, half_open, ALU.add))

            def level_masks():
                dve.wait_ge(const_step, 3 + 14)
                for level in range(1, 7):
                    same = block[:, level, :]
                    if level < 6:
                        ins = nc.vector.tensor_tensor(same, block[:, level + 1, :], same, ALU.subtract)
                    else:
                        ins = nc.vector.tensor_scalar(same, same, -1.0, 1.0, ALU.mult, ALU.add)
                    ins.then_inc(masks_ready, 1)

            tile_dst = [na_q, na_k, na_v, na_z, pre_f, suf_b, hq, i_feat, hz]

            def group(g, first):
                for s in range(IN_SLOTS):
                    split_next(tile_no(g, s), s % RAW)
                    if not first:
                        previous(g, s)
                    elif s == 1:
                        gate_set_up()
                    elif s == 2:
                        level_masks()
                    attention(g, s)
                    dst = tile_dst[s] if s < 9 else at(gates, g * 3 + (s - 9))
                    take_tile(tile_no(g, s), s % 2, dst)

            dve.wait_ge(ss0_ready, 1)
            nc.vector.tensor_scalar(msq[:, 0:1], ssq[:, 0:1], 1.0 / D, EPS, ALU.mult, ALU.add).then_inc(msq_ready, 1)
            dve.wait_ge(x1_landed, 16)
            link(nc.vector.tensor_tensor_reduce(out=xs_tok[:, 1, D // 2:D], in0=x_tok[:, 1, D // 2:D],
                                                in1=x_tok[:, 1, D // 2:D], scale=1.0, scalar=0.0, op0=ALU.mult,
                                                op1=ALU.add, accum_out=ssq[:, 3:4]))
            dve.wait_ge(ss0_ready, 2)
            link(nc.vector.tensor_tensor(ssum[:, 1:2], ssq[:, 2:3], ssq[:, 3:4], ALU.add))
            nc.vector.tensor_scalar(msq[:, 1:2], ssum[:, 1:2], 1.0 / D, EPS, ALU.mult, ALU.add).then_inc(msq_ready, 1)
            for t in range(2):
                dve.wait_ge(rstd_ready, t + 1)
                nc.vector.tensor_scalar(xs_tok[:, t, :], x_tok[:, t, :], rstd[:, t:t + 1], None,
                                        ALU.mult).then_inc(xs_ready, 1)
            dve.wait_ge(vec_ready, 1)
            for i in range(KT):
                if i % 2 == 0:
                    dve.wait_ge(xhi_ready, i + 2)
                nc.vector.scalar_tensor_tensor(out=act_hl[:, i, T:2 * T],
                                               in0=turn_bank[i // 2][:, (i % 2) * T:(i % 2 + 1) * T],
                                               scalar=vec[:, 64 + i:65 + i], in1=act_hl[:, i, 0:T].bitcast(F32),
                                               op0=ALU.mult, op1=ALU.subtract).then_inc(xn_ready, 1)
            dve.wait_ge(lo_ready, 2)
            group(0, True)
            with loop(dve, 1, NG) as g:
                group(g, False)
            for t in range(TAIL):
                n = tile_no(NG, t)
                split_next(n, n % RAW)
                previous(NG, t)
                take_tile(n, t % 2, gates[:, 3 * NG + t, :])
            hgrn_out(NG - 1)
            hgrn_lo(NG - 1)
            dve.wait_ge(gate_ready, 4 * NG)

            def merge(b, j):
                ya, yb = hz, hth
                for i, (y, ps) in enumerate(((ya, ps_proj[b]), (yb, ps_lvl[b]))):
                    dve.wait_ge(part_ready, j * 2 + (N_IN + i + 1))
                    nc.vector.tensor_tensor(y, ps[:, 0:T], part[:, i, :], ALU.add).then_inc(y_step, 1)
                for i, y in enumerate((ya, yb)):
                    dve.wait_ge(y_step, j * 4 + i + 1)
                    nc.vector.scalar_tensor_tensor(out=y, in0=at(gates, j + N_BR * i), scalar=1.0, in1=y,
                                                   op0=ALU.add, op1=ALU.mult).then_inc(y_step, 1)
                dve.wait_ge(y_step, j * 4 + 4)
                nc.vector.tensor_tensor(y_sums[b], ya, yb, ALU.add).then_inc(y_sum, 1)

            def split_y(j, b):
                dve.wait_ge(y_hi, j + 1)
                nc.vector.scalar_tensor_tensor(out=at(act_hl, j)[:, T:2 * T], in0=y_sums[b], scalar=0.5,
                                               in1=at(act_hl, j)[:, 0:T].bitcast(F32), op0=ALU.mult,
                                               op1=ALU.subtract).then_inc(y_ready, 1)

            for r in range(RAW):
                split_next(N_IN + r, r)
                if r:
                    split_y(r - 1, (r - 1) % 2)
                merge(r % 2, r)
            with loop(dve, 1, N_BR // RAW) as jj:
                for r in range(RAW):
                    split_next(jj * RAW + (N_IN + r), r)
                    split_y(jj * RAW + (r - 1), (r - 1) % 2)
                    merge(r % 2, jj * RAW + r)
            split_y(N_BR - 1, 1)

            def weigh(c, t):
                dve.wait_ge(block_sq, c * 2 + t + 1)
                nc.vector.tensor_tensor(block_columns(o_tok[:, t, :], c), at(psum, c * 2 + t),
                                        block_columns(post_w, c), ALU.mult).then_inc(out_taken, 1)

            with loop(dve, 0, LAST_BLOCK) as c:
                for r in range(RAW):
                    split_next(c * RAW + (N_IN + N_BR + r), r)
                dve.wait_ge(tail_landed, 3 * 16)
                for t in range(2):
                    weigh(c, t)
            for r in range(RAW - 1):
                split_next(LAST_BLOCK * RAW + N_IN + N_BR + r, r)

            def out_mean_square(t):
                dve.wait_ge(block_sq, 2 * LAST_BLOCK + t + 1)
                nc.vector.tensor_reduce(ssum[:, t:t + 1], ssq[:, 4 * t:4 * t + 4], AX.X, ALU.add).then_inc(fin_step, 1)
                dve.wait_ge(fin_step, t + 1)
                nc.vector.tensor_scalar(msq[:, t:t + 1], ssum[:, t:t + 1], 1.0 / D, EPS, ALU.mult,
                                        ALU.add).then_inc(msq2_ready, 1)

            def add_residual(t, c):
                v = block_columns(o_tok[:, t, :], c)
                nc.vector.scalar_tensor_tensor(out=v, in0=v, scalar=rstd[:, t:t + 1],
                                               in1=block_columns(x_tok[:, t, :], c), op0=ALU.mult,
                                               op1=ALU.add).then_inc(out_ready, 1)

            out_mean_square(0)
            weigh(LAST_BLOCK, 0)
            dve.wait_ge(rstd2_ready, 1)
            dve.wait_ge(out_taken, 6)
            for c in (0, 1):
                add_residual(0, c)
            out_mean_square(1)
            weigh(LAST_BLOCK, 1)
            dve.wait_ge(rstd2_ready, 2)
            for c in (0, 1, 3):
                if c == 3:
                    dve.wait_ge(out_taken, 8)
                add_residual(1, c)

        @blk.tensor
        def _(pe):
            def project(n, r, sums, operand, between):
                for h in range(2):
                    if h == 1:
                        between()
                    pe.wait_ge(lo_ready, n * 2 + h + 1)
                    i = (2 * r + h) % HALVES
                    for kk in range(8):
                        k = 8 * h + kk
                        first, last = (k == 0, k == KT - 1) if sums[0] is sums[1] else (kk == 0, kk == 7)
                        if isinstance(n, int) and n == 0:
                            pe.wait_ge(xn_ready, max(k + 1, 2))
                            if k % 2 == 0 and k + TURN_AHEAD < KT:
                                turn_x(k + TURN_AHEAD)
                        w = slice(kk * P, (kk + 1) * P)
                        nc.tensor.matmul(sums[h][:, :], w_hi[:, i, w], operand[:, k, :], start=first, stop=False,
                                         skip_group_check=True)
                        ins = nc.tensor.matmul(sums[h][:, 0:T], w_lo[:, i, w], operand[:, k, 0:T], start=False,
                                               stop=last, skip_group_check=True)
                    ins.then_inc(half_used, 1)

            def turn_x(k0):
                if turn_bank[k0 // 2] is ps_tr:
                    pe.wait_ge(vec_ready, 1)
                for k in (k0, k0 + 1):
                    for t in range(2):
                        if k == 0:
                            pe.wait_ge(xs_ready, t + 1)
                        ins = nc.tensor.transpose(turn_bank[k // 2][:, (k % 2) * T + t * P:(k % 2) * T + (t + 1) * P],
                                                  xs_tok[:, t, k * P:(k + 1) * P], block[:, 0, :])
                ins.then_inc(xt_done, 1)

            def head_scores(g, a):
                pe.wait_ge(qk_lo_ready, g + 1)
                wait(pe, s_taken, g * 2 + a)
                rows = slice(HEAD * a, HEAD * (a + 1))
                for u in range(2):
                    t = 1 - u
                    q, k, dst = slice(t * P, (t + 1) * P), slice(T, 2 * T), ps_s[:, u * T:(u + 1) * T]
                    nc.tensor.matmul(dst, qk_hi[rows, q], qk_hi[rows, k], start=True, stop=False)
                    nc.tensor.matmul(dst, qk_hi[rows, q], qk_lo[rows, k], start=False, stop=False)
                    ins = nc.tensor.matmul(dst, qk_lo[rows, q], qk_hi[rows, k], start=False, stop=True)
                ins.then_inc(s_done, 1)

            def turn(v, g, i):
                wait(pe, tr_taken, g * 2 + i)
                for t in range(2):
                    ins = nc.tensor.transpose(ps_tr[:, t * P:(t + 1) * P], v[:, t * P:(t + 1) * P], block[:, 0, :])
                ins.then_inc(tr_done, 1)

            def turn_prob(g, a):
                pe.wait_ge(prob_ready, g * 2 + a + 1)
                wait(pe, pt_taken, g * 2 + a)
                for kt in range(2):
                    for t in range(2):
                        u = 1 - t
                        ins = nc.tensor.transpose(ps_pt[:, kt * T + t * P:kt * T + (t + 1) * P],
                                                  prob[:, a, u * T + kt * P:u * T + (kt + 1) * P], block[:, 0, :])
                ins.then_inc(pt_done, 1)

            def head_out(g, a):
                pe.wait_ge(pt_taken, g * 2 + a + 1)
                pe.wait_ge(tr_taken, g * 2 + 1)
                wait(pe, oa_ready, g)
                for kt in range(2):
                    ins = nc.tensor.matmul(ps_o[HEAD * a:HEAD * (a + 1), 0:T], v_tok[:, kt, HEAD * a:HEAD * (a + 1)],
                                           prob_t[:, a, kt * T:(kt + 1) * T], start=(kt == 0), stop=(kt == 1))
                if a == 1:
                    ins.then_inc(pv_done, 1)

            def level_scores(g, level):
                pe.wait_ge(dec_ready, g * 8 + level + 1)
                wait(pe, lvl_taken, g * 8 + level - 1)
                dst, b = ps_lvl[level % 2], level % 2
                if level == 0:
                    wait(pe, osq_ready, g)
                if level == 1:
                    wait(pe, ob_ready, g)
                for i in range(2):
                    j = 1 - i if level == LEVELS - 1 else i
                    ins = nc.tensor.matmul(dst[:, i * P:(i + 1) * P], k_dec[:, b, i * P:(i + 1) * P],
                                           q_dec[:, b, j * P:(j + 1) * P], start=True, stop=True)
                if level == 0:
                    for i in range(2):
                        c = slice(i * P, (i + 1) * P)
                        ins = nc.tensor.matmul(dst[:, T + i * P:T + (i + 1) * P], key_s[:, c], hq[:, c],
                                               start=True, stop=True)
                ins.then_inc(lvl_done, 1)

            def hgrn_sum(g):
                pe.wait_ge(lvl_taken, g * 8 + 8)
                pe.wait_ge(tr_taken, g * 2 + 2)
                for i in range(2):
                    ins = nc.tensor.matmul(ps_lvl[0][:, 0:T], i_tok[:, i, :], scores_t[:, i * T:(i + 1) * T],
                                           start=(i == 0), stop=(i == 1))
                ins.then_inc(hg_out, 1)

            def square_sum(g):
                pe.wait_ge(osq_ready, g + 1)
                for i in range(2):
                    ins = nc.tensor.matmul(ps_lvl[1][:, i:i + 1], o_sq[:, i * P:(i + 1) * P], ones[:, 0:1],
                                           start=True, stop=True)
                ins.then_inc(ms_done, 1)

            def turn_rst(g):
                pe.wait_ge(rst_spread, g + 1)
                for i in range(2):
                    c = slice(i * P, (i + 1) * P)
                    ins = nc.tensor.transpose(ps_lvl[1][:, c], rst_rows[:, c], block[:, 0, :])
                ins.then_inc(rst_turned, 1)

            def attention(g, s):
                if s == 2:
                    head_scores(g, 0)
                if s == 3:
                    pe.wait_ge(tile_out, tile_no(g, NSLOT_V + 1))
                    turn(na_v, g, 0)
                    head_scores(g, 1)
                if s == 5:
                    turn_prob(g, 0)
                if s == 6:
                    turn_prob(g, 1)
                    head_out(g, 0)
                if s == 7:
                    head_out(g, 1)
                if s == 8:
                    pe.wait_ge(tile_out, tile_no(g, NSLOT_I + 1))
                    turn(i_feat, g, 1)
                if s >= 8:
                    level_scores(g, s - 8)

            def previous(g, s):
                if s < 4:
                    level_scores(g - 1, 4 + s)
                if s == 5:
                    hgrn_sum(g - 1)
                if s == 6:
                    square_sum(g - 1)
                if s == 7:
                    turn_rst(g - 1)

            def group(g, first):
                for s in range(IN_SLOTS):
                    n = tile_no(g, s)
                    wait(pe, tile_out, n - 1)

                    def between():
                        if s == 0:
                            if not first:
                                attention(g - 1, IN_SLOTS - 1)
                        else:
                            if not first:
                                previous(g, s - 1)
                            attention(g, s - 1)

                    project(n, s % RAW, [ps_proj[s % 2]] * 2, act_hl, between)

            pe.wait_ge(x0_landed, 16)
            pe.wait_ge(const_step, 1)
            for _ in range(WARM_UP):
                nc.tensor.matmul(ps_proj[0][:, 0:P], ones[:, :], ones[:, :], start=True, stop=True)
            pe.wait_ge(const_step, 5)
            pe.wait_ge(vec_landed, 4 * 16)
            nc.tensor.transpose(ps_tr[:, 0:88], vec_rows[:, :], block[0:88, 0, 0:88]).then_inc(vec_turned, 1)
            for k in range(0, TURN_AHEAD, 2):
                turn_x(k)

            group(0, True)
            with loop(pe, 1, NG) as g:
                group(g, False)
            for t in range(TAIL):
                n = tile_no(NG, t)
                pe.wait_ge(tile_out, n - 1)
                project(n, n % RAW, [ps_proj[t % 2]] * 2, act_hl,
                        lambda: previous(NG, t - 1) if t else attention(NG - 1, IN_SLOTS - 1))
            previous(NG, TAIL - 1)

            def branch(n, r, j):
                if isinstance(j, int) and j < 2:
                    pe.wait_ge(tile_out, N_IN - 1 + j)
                else:
                    pe.wait_ge(y_sum, j - 1)
                project(n, r, [ps_proj[r % 2], ps_lvl[r % 2]], branch_hl, lambda: pe.wait_ge(ob_lo, NG))

            pe.wait_ge(oa_lo, NG)
            for r in range(RAW):
                branch(N_IN + r, r, r)
            with loop(pe, 1, N_BR // RAW) as jj:
                for r in range(RAW):
                    branch(jj * RAW + (N_IN + r), r, jj * RAW + r)

            def out_sums(c, t, r, h):
                for kk in range(2):
                    k = 4 * r + 2 * h + kk
                    w, i = slice(kk * 512, (kk + 1) * 512), (2 * r + h) % HALVES
                    hi, lo = act_hl[:, k, t * P:(t + 1) * P], act_hl[:, k, T + t * P:T + (t + 1) * P]
                    o = at(psum, c * 2 + t)
                    nc.tensor.matmul(o, hi, w_hi[:, i, w], start=(k == 0), stop=False)
                    nc.tensor.matmul(o, hi, w_lo[:, i, w], start=False, stop=False)
                    ins = nc.tensor.matmul(o, lo, w_hi[:, i, w], start=False, stop=(k == KT - 1))
                return ins

            def column_block(c):
                for r in range(RAW):
                    for h in range(2):
                        pe.wait_ge(lo_ready, c * (2 * RAW) + (2 * (N_IN + N_BR + r) + h + 1))
                        pe.wait_ge(y_ready, 4 * r + 2 * h + 2)
                        if not (c is LAST_BLOCK and r == RAW - 1):
                            for t in range(2):
                                ins = out_sums(c, t, r, h)
                            ins.then_inc(half_used, 1)

            with loop(pe, 0, LAST_BLOCK) as c:
                column_block(c)
            column_block(LAST_BLOCK)
            for t in range(2):
                for h in range(2):
                    ins = out_sums(LAST_BLOCK, t, RAW - 1, h)
                ins.then_inc(half_used, 1)


_INS = ["x", "norm_pre_w", "w_in", "b_gate", "na_rel_bias", "hg_lb_logits", "hg_norm_w", "w_branch", "w_out",
        "norm_post_w"]


def kernel(**inputs):
    import numpy as _np
    import concourse.bacc as _bacc
    from concourse.bass_utils import run_bass_kernel_spmd as _run

    nc = _bacc.Bacc("TRN2", target_bir_lowering=False, num_devices=1)
    arrays, args = {}, []
    for name in _INS:
        a = _np.ascontiguousarray(inputs[name])
        arrays[f"in_{name}"] = a
        args.append(nc.dram_tensor(f"in_{name}", a.shape, mybir.dt.from_np(a.dtype), kind="ExternalInput").ap())
    out = nc.dram_tensor("out_0", (1, T, D), F32, kind="ExternalOutput").ap()
    encoder_layer(nc, *args, out)
    r = _run(nc, [arrays], core_ids=[0])
    return r.results[0]["out_0"]
```
